# Optimizing a Trainium2 kernel written in Bass

```python
import jax, jax.numpy as jnp
from jax import lax
import numpy as np

D_MODEL = 2048
BATCH = 1
SEQ = 512
DEPTH = 1

MIX_WIDTH = D_MODEL
MLSTM_WIDTH = MIX_WIDTH // 2
ATTN_WIDTH = MIX_WIDTH - MLSTM_WIDTH
MLSTM_HEADS = 4
MLSTM_HEAD_DIM = MLSTM_WIDTH // MLSTM_HEADS
MLSTM_CHUNK = 128
CONV_WIDTH = 5
ATTN_HEAD_DIM = 128
ATTN_HEADS = ATTN_WIDTH // ATTN_HEAD_DIM
ATTN_KV_HEADS = 2
ATTN_KV_WIDTH = ATTN_KV_HEADS * ATTN_HEAD_DIM
WINDOW = 128
ATTN_BLOCK = 128
ROPE_THETA = 10000.0
D_FF = -(-(8 * D_MODEL) // (3 * 256)) * 256
N_GATES = 4 * MLSTM_HEADS
IN_PROJ = 4 * MLSTM_WIDTH + N_GATES + ATTN_WIDTH + 2 * ATTN_KV_WIDTH
EPS = 1e-6
NEG_INF = -1e30

kernel_name = 'hymba_mlstm_swa_adaln_block'

def rmsnorm(x, g):
    xf = x.astype(jnp.float32)
    y = xf * lax.rsqrt(jnp.mean(xf * xf, axis=-1, keepdims=True) + EPS)
    return (y * g.astype(jnp.float32)).astype(x.dtype)

def head_layernorm(h):
    mu = jnp.mean(h, axis=-1, keepdims=True)
    hc = h - mu
    return hc * lax.rsqrt(jnp.mean(hc * hc, axis=-1, keepdims=True) + EPS)

def rope(t, positions):
    d = t.shape[-1]
    half = d // 2
    inv = ROPE_THETA ** (-jnp.arange(half, dtype=jnp.float32) * 2.0 / d)
    ang = positions.astype(jnp.float32)[..., None] * inv
    cos = jnp.cos(ang)[:, :, None, :]
    sin = jnp.sin(ang)[:, :, None, :]
    tf = t.astype(jnp.float32)
    t1, t2 = tf[..., :half], tf[..., half:]
    return jnp.concatenate([t1 * cos - t2 * sin, t2 * cos + t1 * sin], axis=-1).astype(t.dtype)

def centred_depthwise_conv(u, w, b):
    C = u.shape[-1]
    pad = CONV_WIDTH // 2
    y = lax.conv_general_dilated(u, w.astype(u.dtype)[:, None, :], window_strides=(1,),
                                 padding=[(pad, pad)], dimension_numbers=('NWC', 'WIO', 'NWC'),
                                 feature_group_count=C)
    return y + b.astype(u.dtype)

def mlstm_chunkwise(q, k, v, log_i, log_f):
    B, H, S, d = q.shape
    L = MLSTM_CHUNK
    nc = S // L

    def to_chunks(t):
        return jnp.moveaxis(t.reshape(t.shape[:2] + (nc, L) + t.shape[3:]), 2, 0)

    xs = (to_chunks(q), to_chunks(k), to_chunks(v), to_chunks(log_i), to_chunks(log_f))
    tri = jnp.tril(jnp.ones((L, L), dtype=bool))

    def step(carry, inp):
        C, n, m = carry
        qj, kj, vj, li, lf = inp
        b = jnp.cumsum(lf, axis=-1)
        dmat = jnp.where(tri, b[..., :, None] - b[..., None, :] + li[..., None, :], NEG_INF)
        inter = b + m[..., None]
        m_t = jnp.maximum(inter, jnp.max(dmat, axis=-1))
        w = jnp.exp(dmat - m_t[..., None])
        a = jnp.exp(inter - m_t)
        qk = jnp.einsum('bhtd,bhsd->bhts', qj, kj) * w
        num = a[..., None] * jnp.einsum('bhtd,bhde->bhte', qj, C) + jnp.einsum('bhts,bhse->bhte', qk, vj)
        den = a * jnp.einsum('bhtd,bhd->bht', qj, n) + jnp.sum(qk, axis=-1)
        h = num / jnp.maximum(jnp.abs(den), jnp.exp(-m_t))[..., None]
        bl = b[..., -1]
        g = bl[..., None] - b + li
        m_new = jnp.maximum(bl + m, jnp.max(g, axis=-1))
        sc = jnp.exp(bl + m - m_new)
        wk = jnp.exp(g - m_new[..., None])[..., None] * kj
        C_new = sc[..., None, None] * C + jnp.einsum('bhsd,bhse->bhde', wk, vj)
        n_new = sc[..., None] * n + jnp.sum(wk, axis=-2)
        return (C_new, n_new, m_new), h

    init = (jnp.zeros((B, H, d, d), jnp.float32), jnp.zeros((B, H, d), jnp.float32),
            jnp.zeros((B, H), jnp.float32))
    _, hs = lax.scan(step, init, xs)
    return jnp.moveaxis(hs, 0, 2).reshape(B, H, S, d)

def windowed_gqa(q, k, v, sink):
    B, S, H, d = q.shape
    G = k.shape[2]
    R = H // G
    blk = ATTN_BLOCK
    nb = S // blk
    qb = q.reshape(B, nb, blk, G, R, d)
    pad = ((0, 0), (blk, blk), (0, 0), (0, 0))
    kp = jnp.pad(k, pad).reshape(B, nb + 2, blk, G, d)
    vp = jnp.pad(v, pad).reshape(B, nb + 2, blk, G, d)
    kb = jnp.concatenate([kp[:, :-2], kp[:, 1:-1], kp[:, 2:]], axis=2)
    vb = jnp.concatenate([vp[:, :-2], vp[:, 1:-1], vp[:, 2:]], axis=2)
    s = jnp.einsum('bnqgrd,bnkgd->bngrqk', qb, kb).astype(jnp.float32) * (d ** -0.5)
    qpos = jnp.arange(nb)[:, None] * blk + jnp.arange(blk)[None, :]
    kpos = (jnp.arange(nb)[:, None] - 1) * blk + jnp.arange(3 * blk)[None, :]
    rel = kpos[:, None, :] - qpos[:, :, None]
    valid = (jnp.abs(rel) <= WINDOW) & (kpos[:, None, :] >= 0) & (kpos[:, None, :] < S)
    s = jnp.where(valid[None, :, None, None, :, :], s, NEG_INF)
    sink_l = jnp.broadcast_to(sink.astype(jnp.float32).reshape(G, R)[None, None, :, :, None, None],
                              s.shape[:-1] + (1,))
    p = jax.nn.softmax(jnp.concatenate([s, sink_l], axis=-1), axis=-1)[..., :-1]
    o = jnp.einsum('bngrqk,bnkgd->bnqgrd', p.astype(v.dtype), vb)
    return o.reshape(B, S, H, d)

def hybrid_mixer(h, positions, w_in, b_gates, w_conv, b_conv, g_mlstm_out, sink, g_attn_out, w_out):
    B, S, _ = h.shape
    f32 = jnp.float32
    proj = h @ w_in.astype(h.dtype)
    sizes = [MLSTM_WIDTH, MLSTM_WIDTH, MLSTM_WIDTH, MLSTM_WIDTH, N_GATES, ATTN_WIDTH, ATTN_KV_WIDTH]
    cuts = [int(v) for v in np.cumsum(sizes)]
    mq, mk, mv, mo, gpre, aq, ak, av = jnp.split(proj, cuts, axis=-1)

    qk = jax.nn.silu(centred_depthwise_conv(jnp.concatenate([mq, mk], axis=-1), w_conv, b_conv))
    mq, mk = jnp.split(qk, 2, axis=-1)

    def heads(t):
        return t.reshape(B, S, MLSTM_HEADS, MLSTM_HEAD_DIM).transpose(0, 2, 1, 3).astype(f32)

    q = heads(mq)
    k = heads(mk) * (MLSTM_HEAD_DIM ** -0.5)
    v = heads(mv)
    gates = (gpre.astype(f32) + b_gates.astype(f32)).reshape(B, S, 4, MLSTM_HEADS).transpose(2, 0, 3, 1)
    li_f, lf_f = gates[0], jax.nn.log_sigmoid(gates[1])
    li_b, lf_b = gates[2], jax.nn.log_sigmoid(gates[3])
    h_fwd = mlstm_chunkwise(q, k, v, li_f, lf_f)
    flip = lambda t: jnp.flip(t, axis=2)
    h_bwd = flip(mlstm_chunkwise(flip(q), flip(k), flip(v), flip(li_b), flip(lf_b)))
    hm = head_layernorm(h_fwd + h_bwd).transpose(0, 2, 1, 3).reshape(B, S, MLSTM_WIDTH)
    m_out = (jax.nn.sigmoid(mo.astype(f32)) * hm * g_mlstm_out.astype(f32)).astype(h.dtype)

    aq = rope(aq.reshape(B, S, ATTN_HEADS, ATTN_HEAD_DIM), positions)
    ak = rope(ak.reshape(B, S, ATTN_KV_HEADS, ATTN_HEAD_DIM), positions)
    av = av.reshape(B, S, ATTN_KV_HEADS, ATTN_HEAD_DIM)
    a_out = windowed_gqa(aq, ak, av, sink).reshape(B, S, ATTN_WIDTH)
    a_out = rmsnorm(a_out, g_attn_out)

    return jnp.concatenate([m_out, a_out], axis=-1) @ w_out.astype(h.dtype)

def swiglu(h, w_gate, w_up, w_down):
    return (jax.nn.silu(h @ w_gate.astype(h.dtype)) * (h @ w_up.astype(h.dtype))) @ w_down.astype(h.dtype)

def setup_inputs(seed: int = 0) -> dict:
    key = jax.random.key(seed)
    ks = jax.random.split(key, 20)
    f32 = jnp.float32
    s_d = D_MODEL ** -0.5
    x = jax.random.normal(ks[0], (BATCH, SEQ, D_MODEL), f32)
    c = jax.random.normal(ks[1], (BATCH, D_MODEL), f32)
    positions = (jnp.arange(SEQ, dtype=jnp.int32)[None, :]
                 + jax.random.randint(ks[2], (BATCH, 1), 0, 4096, dtype=jnp.int32))
    w_ada = jax.random.normal(ks[3], (DEPTH, D_MODEL, 6 * D_MODEL), f32) * s_d
    b_ada = 0.02 * jax.random.normal(ks[4], (DEPTH, 6 * D_MODEL), f32)
    g_norm1 = 1.0 + 0.02 * jax.random.normal(ks[5], (DEPTH, D_MODEL), f32)
    g_norm2 = 1.0 + 0.02 * jax.random.normal(ks[6], (DEPTH, D_MODEL), f32)
    w_in = jax.random.normal(ks[7], (DEPTH, D_MODEL, IN_PROJ), f32) * s_d
    f_bias = jnp.linspace(3.0, 6.0, MLSTM_HEADS, dtype=f32)
    zero_b = jnp.zeros((MLSTM_HEADS,), f32)
    base = jnp.concatenate([zero_b, f_bias, zero_b, f_bias])
    b_gates = base[None, :] + 0.1 * jax.random.normal(ks[8], (DEPTH, N_GATES), f32)
    w_conv = jax.random.normal(ks[9], (DEPTH, CONV_WIDTH, 2 * MLSTM_WIDTH), f32) * (CONV_WIDTH ** -0.5)
    b_conv = 0.02 * jax.random.normal(ks[10], (DEPTH, 2 * MLSTM_WIDTH), f32)
    g_mlstm_out = 1.0 + 0.02 * jax.random.normal(ks[11], (DEPTH, MLSTM_WIDTH), f32)
    sink = 0.5 * jax.random.normal(ks[12], (DEPTH, ATTN_HEADS), f32)
    g_attn_out = 1.0 + 0.02 * jax.random.normal(ks[13], (DEPTH, ATTN_WIDTH), f32)
    w_out = jax.random.normal(ks[14], (DEPTH, MIX_WIDTH, D_MODEL), f32) * (MIX_WIDTH ** -0.5)
    w_gate = jax.random.normal(ks[15], (DEPTH, D_MODEL, D_FF), f32) * s_d
    w_up = jax.random.normal(ks[16], (DEPTH, D_MODEL, D_FF), f32) * s_d
    w_down = jax.random.normal(ks[17], (DEPTH, D_FF, D_MODEL), f32) * (D_FF ** -0.5)
    g_final = 1.0 + 0.02 * jax.random.normal(ks[18], (D_MODEL,), f32)
    return {'x': x, 'c': c, 'positions': positions, 'w_ada': w_ada, 'b_ada': b_ada,
            'g_norm1': g_norm1, 'g_norm2': g_norm2, 'w_in': w_in, 'b_gates': b_gates,
            'w_conv': w_conv, 'b_conv': b_conv, 'g_mlstm_out': g_mlstm_out, 'sink': sink,
            'g_attn_out': g_attn_out, 'w_out': w_out, 'w_gate': w_gate, 'w_up': w_up,
            'w_down': w_down, 'g_final': g_final}

def reference(x, c, positions, w_ada, b_ada, g_norm1, g_norm2, w_in, b_gates, w_conv, b_conv,
              g_mlstm_out, sink, g_attn_out, w_out, w_gate, w_up, w_down, g_final):
    for l in range(DEPTH):
        mod = jax.nn.silu(c) @ w_ada[l].astype(c.dtype) + b_ada[l].astype(c.dtype)
        sh1, sc1, gt1, sh2, sc2, gt2 = [t[:, None, :] for t in jnp.split(mod, 6, axis=-1)]
        h = rmsnorm(x, g_norm1[l]) * (1.0 + sc1) + sh1
        x = x + gt1 * hybrid_mixer(h, positions, w_in[l], b_gates[l], w_conv[l], b_conv[l],
                                   g_mlstm_out[l], sink[l], g_attn_out[l], w_out[l])
        h = rmsnorm(x, g_norm2[l]) * (1.0 + sc2) + sh2
        x = x + gt2 * swiglu(h, w_gate[l], w_up[l], w_down[l])
    return rmsnorm(x, g_final)


_drawn_inputs = setup_inputs


def setup_inputs(seed=0):
    import zlib

    import numpy as np

    out = dict(_drawn_inputs(seed))
    spreads = {}
    factors = {'g_norm1': 8.0,
     'g_norm2': 4.296,
     'b_conv': 8.0,
     'g_mlstm_out': 8.0,
     'sink': 8.0,
     'g_attn_out': 6.919,
     'g_final': 2.819}
    for name, (base, spread) in spreads.items():
        noise = np.random.default_rng([zlib.crc32(name.encode()), seed]).standard_normal(out[name].shape)
        drawn = base * np.exp(spread * noise) if base else spread * noise
        out[name] = __import__('jax').numpy.asarray(drawn.astype(out[name].dtype))
    for name, factor in factors.items():
        out[name] = (out[name] * factor).astype(out[name].dtype)
    return out
```

```python
from contextlib import ExitStack

import numpy as np
import concourse.bass as bass
from concourse import mybir

F32 = mybir.dt.float32
F32R = mybir.dt.float32r
I32 = mybir.dt.int32
ALU = mybir.AluOpType
ACT = mybir.ActivationFunctionType
AX = mybir.AxisListType

P = 128
D = 2048
S = 512
KT = D // P
TB = S // P
HEADS = 4
HD = 256
CONV = 5
AH = 8
AD = 128
GATES = 16
FF = 5632
CH = 512
NCH = FF // CH
SLOT = 2048
EPS = 1e-6
NEG = -1e30
MAGIC = 1.5 * 2.0 ** 23
TWO_PI = 2.0 * np.pi
PI_1 = 6.28125
PI_2 = float(np.round((TWO_PI - PI_1) * 2.0 ** 20) / 2.0 ** 20)
PI_3 = float(np.float32(TWO_PI - PI_1 - PI_2))
PI_SAFE = 3.1415925
COL_AK = 4 * 1024 + GATES + 1024
COL_AV = COL_AK + 256
COL_G = 4 * 1024
COL_AQ = COL_G + GATES

C_G1, C_G2, C_GF, C_BC, C_GM, C_GA, C_C, C_BA, C_WC, C_END = 0, 16, 32, 48, 64, 72, 80, 96, 192, 272

PAIRS = [(i, j) for i in range(TB) for j in range(i + 1)]
PAIR = {p: n for n, p in enumerate(PAIRS)}
GR = 36


class Chain:

    def __init__(self, eng, sem):
        self.eng, self.sem, self.base, self.n = eng, sem, 0, 0

    def link(self, ins):
        ins.then_inc(self.sem, 1)
        self.n += 1
        self.eng.wait_ge(self.sem, self.base + self.n)

    def enter(self, iteration, first, each):
        self.start, self.each = self.base + self.n, each
        self.base, self.n = iteration * each + (self.start - first * each), 0

    def leave(self, times):
        assert self.n == self.each, (self.n, self.each)
        self.base, self.n = self.start + self.each * times, 0


def program(nc, x, c, positions, w_ada, b_ada, g1, g2, w_in, b_gates, w_conv, b_conv, gm, sink, ga,
            w_out, w_gate, w_up, w_down, gf, rope_inv, out):
    ctx = ExitStack()
    with ctx:
        top = [16512]

        def at(name, shape, dt, off):
            return nc.alloc_sbuf_tensor_at(name, shape, dt, offset=off)

        def size(shape):
            n = 4
            for k in shape[1:]:
                n *= k
            return (n + 31) // 32 * 32

        def sb(name, shape, dt=F32):
            off = top[0]
            top[0] += size(shape)
            return at(name, shape, dt, off)

        def region(base, names):
            got, off = [], base
            for name, shape, dt in names:
                got.append(at(name, shape, dt, off))
                off += size(shape)
            return got, off

        ident = sb("ident", [P, P])
        mask3 = sb("mask3", [P, 3 * P])
        ones = sb("ones", [P, P])
        cols = sb("cols", [P, C_END])
        modp = sb("modp", [P, 12, KT])
        mod = sb("mod", [P, 6, KT])
        csil = sb("csil", [P, KT])
        acol = sb("acol", [P, 14 * GR])
        mnat = sb("mnat", [64, S])
        sel2 = sb("sel2", [64, 2, P])
        sinkb = sb("sinkb", [P, AH])
        nsink = sb("nsink", [P, AH])
        bgate = sb("bgate", [GATES, 1])
        invf = sb("invf", [P, 2])
        tiny = sb("tiny", [P, 64])
        cosT = sb("cosT", [P, S])
        sinT = sb("sinT", [P, S])
        mask_up, mask_lo = mask3[:, 0:P], mask3[:, 2 * P:3 * P]
        ssq, rsx, halfneg, dd, rr, mv, ve, rs, st6 = (
            tiny[:, 0:4], tiny[:, 4:8], tiny[:, 8:12], tiny[:, 12:14], tiny[:, 14:16], tiny[:, 16:24],
            tiny[:, 24:28], tiny[:, 28:32], tiny[:, 32:38])
        halfpi = tiny[:, 38:39]
        wraw = [sb(f"wraw{i}", [P, SLOT]) for i in range(2)]
        whi = [sb(f"whi{i}", [P, SLOT], F32R) for i in range(2)]
        wlo = [sb(f"wlo{i}", [P, SLOT], F32R) for i in range(2)]
        araw_off = top[0]
        araw = [sb(f"araw{i}", [P, D]) for i in range(2)]
        acc = sb("acc", [P, D])
        big = top[0]
        top[0] += 2 * KT * S * 4
        (h_hi, h_lo), _ = region(big, [("h_hi", [P, KT, S], F32R), ("h_lo", [P, KT, S], F32R)])
        (o_hi, o_lo), _ = region(big, [("o_hi", [P, KT, S], F32R), ("o_lo", [P, KT, S], F32R)])
        (f_hi, f_lo), _ = region(big, [("f_hi", [P, KT, S], F32R), ("f_lo", [P, KT, S], F32R)])
        (yout, gfb), _ = region(big, [("yout", [P, TB, D], F32), ("gfb", [P, D], F32)])
        mix = top[0]
        (mT, qk, convin, sigo, vT, V, Pt, Et, bc, md), end1 = region(mix, [
            ("mT", [P, 8, S], F32), ("qk", [P, 4, S], F32), ("convin", [P, 4, S + 4], F32),
            ("sigo", [P, 2, S], F32), ("vT", [P, 2, S], F32), ("V", [P, TB, HD + 1], F32),
            ("Pt", [P, 2, 5, P], F32), ("Et", [P, 5, P], F32), ("bc", [P, 2, S], F32), ("md", [P, 2, P], F32)])
        vT_off = mix + size([P, 8, S]) + size([P, 4, S]) + size([P, 4, S + 4]) + size([P, 2, S])
        (hm,), _ = region(vT_off, [("hm", [P, TB, HD], F32)])
        (xnT, xst0, xst1, hf), end0 = region(mix, [
            ("xnT", [P, KT, S], F32), ("xst0", [P, D], F32), ("xst1", [P, D], F32), ("hf", [P, 2, S], F32)])
        xst = [xst0, xst1]
        (stg, posi, ang, kf, ar2, junk), _ = region(big, [
            ("stg", [P, 3, P], F32), ("posi", [P, S], I32), ("ang", [P, S], F32), ("kf", [P, S], F32),
            ("ar2", [P, S], F32), ("junk", [P, D], F32)])
        (gsb, selI, selZ, li, zz, az, bb, aa, mx, blm, arow), end2 = region(mix, [
            ("gsb", [GATES, S], F32), ("selI", [GATES, 64], F32), ("selZ", [GATES, 64], F32),
            ("li", [64, S], F32), ("zz", [64, S], F32), ("az", [64, S], F32), ("bb", [64, S], F32),
            ("aa", [64, S], F32), ("mx", [64, S], F32), ("blm", [64, 16], F32), ("arow", [64, 10, P], F32)])
        (aout,), _ = region(mix, [("aout", [P, TB, AH * AD], F32)])
        (sc, pr, prT, sm, ajunk), _ = region(big + 8 * S * 4, [
            ("sc", [P, 2, 3 * P], F32), ("pr", [P, 2, 3 * P], F32), ("prT", [P, 2, 3 * P], F32),
            ("sm", [P, 32, 4], F32), ("ajunk", [P, AH * AD], F32)])
        (xT, xs0, xs1, sqt, ssum), end3 = region(mix, [
            ("xT", [P, KT, S], F32), ("xs0", [P, TB, S], F32), ("xs1", [P, TB, S], F32),
            ("sqt", [P, 2, S], F32), ("ssum", [P, S], F32)])
        (ht, hu), _ = region(mix + size([P, KT, S]), [("ht", [P, 2, S], F32), ("hu", [P, 2, S], F32)])
        xs = [xs0, xs1]
        a_hi = at("a_hi", [P, 4, S], F32R, araw_off)
        a_lo = at("a_lo", [P, 4, S], F32R, araw_off + 4 * S * 4)
        gs = at("gs", [P, 4, S], F32, araw_off + 8 * S * 4)

        assert max(end0, end1, end2, end3) <= 229344, (top[0], end0, end1, end2, end3)

        ps = [ctx.enter_context(nc.psum_tensor(f"ps{i}", [P, S], F32)) for i in range(8)]

        def sem(name):
            return ctx.enter_context(nc.semaphore(name))


        const_ld, x_ld, masks_ok, cst_T, cst_ok = map(sem, ["const_ld", "x_ld", "masks_ok", "cst_T", "cst_ok"])
        x_ld = [x_ld, sem("x_ld1")]
        ssq_ok, ms_ok, rsx_ok, xn_ok, xT_ps, xT_sb = map(
            sem, ["ssq_ok", "ms_ok", "rsx_ok", "xn_ok", "xT_ps", "xT_sb"])
        silu_sig, silu_ok, trig_in, trig_ok = map(sem, ["silu_sig", "silu_ok", "trig_in", "trig_ok"])
        ada_ld = [sem(f"ada_ld{i}") for i in range(4)]
        ada_acc, ada_sum, modp_ok, mod_ok = map(sem, ["ada_acc", "ada_sum", "modp_ok", "mod_ok"])
        hhi_ok, hlo_ok = map(sem, ["hhi_ok", "hlo_ok"])
        w_ld = [sem("w_ld0"), sem("w_ld1")]
        whi_ok, wlo_ok, w_used = map(sem, ["whi_ok", "wlo_ok", "w_used"])
        gate_sb, gate_sel, gate_rows, gate_exp, gate_ln, arow_ok, gcol_ps, gcol_sb, em_ok = map(
            sem, ["gate_sb", "gate_sel", "gate_rows", "gate_exp", "gate_ln", "arow_ok", "gcol_ps",
                  "gcol_sb", "em_ok"])
        proj_sb, conv_pre, conv_sig, conv_ok, vtr_ps, v_ok = map(
            sem, ["proj_sb", "conv_pre", "conv_sig", "conv_ok", "vtr_ps", "v_ok"])
        sel_ok, bc_ps, bc_sb, md_ok, s_ps, e_ok, p_ok, num_ps, num_used = map(
            sem, ["sel_ok", "bc_ps", "bc_sb", "md_ok", "s_ps", "e_ok", "p_ok", "num_ps", "num_used"])
        var_ok, rs_ok, hn_ok, ht_ps, mT_ok = map(sem, ["var_ok", "rs_ok", "hn_ok", "ht_ps", "mT_ok"])
        rot_ok, rope_ok = map(sem, ["rot_ok", "rope_ok"])
        as_ps, nm_ok, ex_ok, es_ok, pt_ps, pt_sb, pv_ps, ao_ok = map(
            sem, ["as_ps", "nm_ok", "ex_ok", "es_ok", "pt_ps", "pt_sb", "pv_ps", "ao_ok"])
        assq_ok, ams_ok, ars_ok, aon_ok, at_ps, ohi_ok, olo_ok, mhi_ok, mlo_ok = map(
            sem, ["assq_ok", "ams_ok", "ars_ok", "aon_ok", "at_ps", "ohi_ok", "olo_ok", "mhi_ok", "mlo_ok"])
        v_ld = [sem("v_ld0"), sem("v_ld1")]
        xs_ld = [sem("xs_ld0"), sem("xs_ld1")]
        vhi_ok, vlo_ok, v_used = map(sem, ["vhi_ok", "vlo_ok", "v_used"])
        c_sb, ct_ps, c_add, sq_ok, ssum_ok, ssum0 = map(
            sem, ["c_sb", "ct_ps", "c_add", "sq_ok", "ssum_ok", "ssum0"])
        n_ps, n_ms, n_rs, n_dg, n_bc, n_mul, fhi_ok, flo_ok = map(
            sem, ["n_ps", "n_ms", "n_rs", "n_dg", "n_bc", "n_mul", "fhi_ok", "flo_ok"])
        f_free, sig_ok, ahi_ok, alo_ok = map(sem, ["f_free", "sig_ok", "ahi_ok", "alo_ok"])
        yt_ps, y_sb, gf_ld, y_ok, y_okb, y_out = map(sem, ["yt_ps", "y_sb", "gf_ld", "y_ok", "y_okb", "y_out"])
        dve_chain, pool_chain = map(sem, ["dve_chain", "pool_chain"])

        NB = 45
        NC_, ND = 16, 132
        HALF0 = [(0, 0), (0, 1), (1, 0), (1, 1)]
        ROPE = [convin[:, i, 2:2 + S] for i in range(4)] + [sigo[:, i, :] for i in range(2)] + \
               [qk[:, i, :] for i in range(4)]
        QH, KG = ROPE[2:], ROPE[:2]
        UNITS = [(n, h) for h in range(AH) for n in range(TB)]

        def blocks(n):
            return [k for k in (n - 1, n, n + 1) if 0 <= k < TB]

        def tile_done(h, g, i):
            return h * 16 + (4 * g + 5 + i)

        def w3(t, k):
            return t[:].rearrange("p (k c) -> p k c", k=k)

        block = ctx.enter_context(nc.Block())

        @block.sync
        def _(sp):
            def rows(v, b=P):
                return v.rearrange("o (a b) -> (o a) b", b=b)

            for dst, src in ((stg[C_G1:C_G1 + 16, 0, :], rows(g1)), (stg[C_G2:C_G2 + 16, 0, :], rows(g2)),
                             (stg[C_GF:C_GF + 16, 0, :], gf.rearrange("(a b) -> a b", b=P)),
                             (stg[C_BC:C_BC + 16, 0, :], rows(b_conv)), (stg[C_GM:C_GM + 8, 0, :], rows(gm)),
                             (stg[C_GA:C_GA + 8, 0, :], rows(ga)), (stg[C_C:C_C + 16, 0, :], rows(c)),
                             (stg[0:96, 1, :], rows(b_ada)),
                             (stg[0:80, 2, :], w_conv.rearrange("o k (a b) -> (o k a) b", b=P)),
                             (sinkb[:], sink[0, :].partition_broadcast(P)),
                             (bgate[:], b_gates.rearrange("o g -> g o")),
                             (posi[:], positions[0, :].partition_broadcast(P)),
                             (invf[:], rope_inv)):
                sp.dma_start(dst, src).then_inc(const_ld, 16)

            def ada_src(q, kt):
                return w_ada[0, kt * P:(kt + 1) * P, q * D:(q + 1) * D]

            ring0 = [wraw[0], wraw[1], araw[0], araw[1]]
            n = 0
            for q, half in HALF0:
                for j in range(8):
                    if n >= 4:
                        sp.wait_ge(ada_acc, n - 3)
                    sp.dma_start(ring0[n % 4][:], ada_src(q, 8 * half + j)).then_inc(ada_ld[n % 4], 16)
                    if n % 4 == 0 and n // 4 < TB:
                        tb = n // 4
                        if tb >= 2:
                            sp.wait_ge(xT_ps, 4 * (tb - 1))
                        sp.dma_start(xst[tb % 2][:], x[0, tb * P:(tb + 1) * P, :]).then_inc(x_ld[tb % 2], 16)
                    n += 1

            def w_slot(par, s, col0, kk, first=False):
                if not first:
                    sp.wait_ge(wlo_ok, s - 1)
                sp.dma_start(w3(wraw[par], 8), w_in[0, kk * 1024:(kk + 1) * 1024, col0].rearrange(
                    "(k p) c -> p k c", p=P)).then_inc(w_ld[par], 16)

            def ada_slot(par, m, q, kt, wait=True):
                sp.wait_ge(ada_acc, 32 + m - 1)
                sp.dma_start(araw[par][:], w_ada[0, kt * P:(kt + 1) * P, q]).then_inc(ada_ld[2 + par], 16)

            sp.wait_ge(ada_acc, 29)
            sp.dma_start(w3(wraw[0], 16), w_in[0, :, COL_G:COL_G + P].rearrange("(k p) c -> p k c", p=P))\
                .then_inc(w_ld[0], 16)
            sp.wait_ge(ada_acc, 30)
            w_slot(1, 1, slice(0, 256), 0, first=True)

            def body(h, cols_of, q_cols, kt0, steps=8, start=0):
                for j in range(start, steps + 1):
                    if j < steps:
                        w_slot((1 + j) % 2, h * 8 + (1 + j), cols_of(j // 2), j % 2)
                    if j > 0:
                        ada_slot((j - 1) % 2, h * 8 + (j - 1), q_cols, kt0 + j - 1)

            body(0, lambda g: slice(g * 1024, g * 1024 + 256), slice(2 * D, 3 * D), 0, start=1)
            with sp.Fori(1, HEADS) as h:
                body(h, lambda g: bass.ds(h * 256 + g * 1024, 256), bass.ds(h * D + 2 * D, D), 0)
            tail = [COL_AK, COL_AQ, COL_AV, COL_AQ + 256]
            body(4, lambda g: slice(tail[g], tail[g] + 256), slice(2 * D, 3 * D), 8)
            for j in range(5):
                if j < 4:
                    w_slot((1 + j) % 2, 41 + j, slice(COL_AQ + 512 + (j // 2) * 256, COL_AQ + 768 + (j // 2) * 256), j % 2)
                for i in range(2 if j else 0):
                    ada_slot(i, 40 + 2 * (j - 1) + i, slice(3 * D, 4 * D), 8 + 2 * (j - 1) + i)

            def v_load(par, v, w, krow, col, wait=True):
                if wait:
                    sp.wait_ge(vlo_ok, v - 1)
                sp.dma_start(w3(wraw[par], 4), w[0, krow, col].rearrange("(k p) c -> p k c", p=P))\
                    .then_inc(v_ld[par], 16)

            for v in range(NC_):
                u, ks = v // 4, v % 4
                if v < 2:
                    sp.wait_ge(wlo_ok, NB)
                v_load(v % 2, v, w_out, slice(ks * 512, ks * 512 + 512), slice(u * 512, u * 512 + 512), v >= 2)
                ada_slot(v % 2, 48 + v, slice((4 + v // 8) * D, (5 + v // 8) * D), 8 + v % 8)
                if ks == 2:
                    if u < 2:
                        sp.wait_ge(at_ps, 8)
                    else:
                        sp.wait_ge(ct_ps, u - 1)
                    sp.dma_start(xs[u % 2][:], x[0, :, u * 512:u * 512 + 512].rearrange("(b p) c -> p b c", p=P))\
                        .then_inc(xs_ld[u % 2], 16)

            def gu(v0, w, col):
                for ks in range(4):
                    v_load(ks % 2, v0 + ks, w, slice(ks * 512, ks * 512 + 512), col)

            def dn(v0, krow):
                for u in range(4):
                    v_load(u % 2, v0 + u, w_down, krow, slice(u * 512, u * 512 + 512))

            gu(16, w_gate, slice(0, CH))
            gu(20, w_up, slice(0, CH))
            with sp.Fori(0, NCH - 1) as i:
                gu(i * 12 + 24, w_gate, bass.ds(i * CH + CH, CH))
                dn(i * 12 + 28, bass.ds(i * CH, CH))
                gu(i * 12 + 32, w_up, bass.ds(i * CH + CH, CH))
            dn(NC_ + 8 + 12 * (NCH - 1), slice((NCH - 1) * CH, NCH * CH))
            sp.wait_ge(v_used, 4 * 144)
            sp.dma_start(gfb[:], gf.partition_broadcast(P)).then_inc(gf_ld, 16)
            for tb in range(TB):
                if tb < 2:
                    sp.wait_ge(y_ok, tb + 1)
                else:
                    sp.wait_ge(y_okb, tb - 1)
                sp.dma_start(out[0, tb * P:(tb + 1) * P, :], yout[:, tb, :]).then_inc(y_out, 16)
            sp.wait_ge(y_out, 16 * TB)

        @block.gpsimd
        def _(pool):
            ch = Chain(pool, pool_chain)
            ch.link(pool.memset(ident[:], 0.0))
            ch.link(pool.memset(mask3[:], 0.0))
            pool.affine_select(out=ident[:], in_=ident[:], compare_op=ALU.not_equal, fill=1.0, base=0,
                               pattern=[[-1, P]], channel_multiplier=1).then_inc(masks_ok, 1)
            pool.affine_select(out=mask_up, in_=mask_up, compare_op=ALU.is_ge, fill=NEG, base=0,
                               pattern=[[1, P]], channel_multiplier=-1).then_inc(masks_ok, 1)
            pool.affine_select(out=mask_lo, in_=mask_lo, compare_op=ALU.is_ge, fill=NEG, base=0,
                               pattern=[[-1, P]], channel_multiplier=1).then_inc(masks_ok, 1)
            pool.memset(ones[:], 1.0).then_inc(masks_ok, 1)
            ch.link(pool.memset(halfneg, -0.5))
            pool.memset(halfpi, np.pi / 2).then_inc(masks_ok, 1)

            for tb in range(TB):
                pool.wait_ge(ms_ok, tb + 1)
                pool.tensor_tensor(rsx[:, tb:tb + 1], rsx[:, tb:tb + 1], halfneg[:, 0:1], ALU.pow).then_inc(rsx_ok, 1)

            def lo(s, par):
                pool.wait_ge(whi_ok, s + 1)
                pool.tensor_tensor(wlo[par][:], wraw[par][:], whi[par][:].bitcast(F32), ALU.subtract)\
                    .then_inc(wlo_ok, 1)

            def body(h, mixing, steps=8, last=NB):
                for j in range(steps):
                    if not isinstance(h, int) or 3 + 8 * h + j < last:
                        lo(3 + 8 * h + j, (1 + j) % 2)
                    if mixing and j == 4:
                        pool.wait_ge(var_ok, h)
                        pool.tensor_tensor(rs, ve, halfneg, ALU.pow).then_inc(rs_ok, 1)

            for s in range(3):
                lo(s, s % 2)
            body(0, False)
            with pool.Fori(1, HEADS) as h:
                body(h, True)
            body(4, True)
            body(5, False, steps=4)

            pool.wait_ge(ams_ok, 1)
            pool.tensor_tensor(rs, ve, halfneg, ALU.pow).then_inc(ars_ok, 1)

            def add_squares(n0, count, start):
                for n in range(count):
                    pool.wait_ge(sq_ok, n0 + n + 1)
                    if n == 0:
                        pool.tensor_copy(ssum[:], sqt[:, 0, :]).then_inc(ssum_ok, 1)
                    else:
                        pool.wait_ge(ssum_ok, n0 + n)
                        pool.tensor_tensor(ssum[:], ssum[:], sqt[:, n % 2, :], ALU.add).then_inc(ssum_ok, 1)

            def power(k):
                pool.wait_ge(n_ms, k)
                pool.tensor_tensor(rs, ve, halfneg, ALU.pow).then_inc(n_rs, 1)

            add_squares(0, KT, 0)
            power(1)
            add_squares(KT, KT, 0)
            power(2)

        @block.scalar
        def _(act):
            A = nc.scalar.activation
            act.wait_ge(cst_ok, 1)
            A(tiny[:, 40:56], cols[:, C_C:C_C + 16], ACT.Sigmoid).then_inc(silu_sig, 1)
            for tb in range(TB):
                act.wait_ge(x_ld[tb % 2], 16 * (tb // 2 + 1))
                if tb:
                    act.wait_ge(ssq_ok, tb)
                A(junk[:], xst[tb % 2][:], ACT.Square, accum_out=ssq[:, tb:tb + 1]).then_inc(ssq_ok, 1)
                for q in range(4):
                    act.wait_ge(xT_ps, 4 * tb + q + 1)
                    A(xnT[:, 4 * q:4 * q + 4, tb * P:(tb + 1) * P],
                      ps[q % 2][:].rearrange("p (k t) -> p k t", k=4), ACT.Copy).then_inc(xT_sb, 1)
            act.wait_ge(trig_in, 1)
            A(sinT[:], ang[:], ACT.Sin, scale=invf[:, 1:2]).then_inc(trig_ok, 1)
            A(ar2[:], ang[:], ACT.Abs).then_inc(trig_ok, 1)
            act.wait_ge(trig_ok, 2)
            A(cosT[:], ar2[:], ACT.Sin, scale=-1.0, bias=halfpi).then_inc(trig_ok, 1)

            def hi(s, par, cnt):
                act.wait_ge(w_ld[par], 16 * cnt)
                A(whi[par][:], wraw[par][:], ACT.Copy).then_inc(whi_ok, 1)

            hi(0, 0, 1)
            hi(1, 1, 1)
            act.wait_ge(mod_ok, 1)
            act.wait_ge(trig_ok, 3)
            for kt in range(KT):
                A(h_hi[:, kt, :], xnT[:, kt, :], ACT.Identity, scale=mod[:, 1, kt:kt + 1],
                  bias=mod[:, 0, kt:kt + 1]).then_inc(hhi_ok, 1)
            act.wait_ge(w_used, 2)
            hi(2, 0, 2)

            def gates():
                act.wait_ge(gate_rows, 1)
                A(az[:], az[:], ACT.Sigmoid).then_inc(gate_exp, 1)
                act.wait_ge(gate_exp, 1)
                A(az[:], az[:], ACT.Ln).then_inc(gate_ln, 1)
            def exp_minus_m():
                act.wait_ge(gcol_sb, 1)
                A(acol[:, 10 * GR:14 * GR], acol[:, 10 * GR:14 * GR], ACT.Exp, scale=-1.0).then_inc(em_ok, 1)



            def evac(dst, bank, n):
                act.wait_ge(w_used, n)
                A(dst, ps[bank][:], ACT.Copy).then_inc(proj_sb, 1)

            def o_gate(h, kind):
                if kind == "head" and not (isinstance(h, int) and h == 0):
                    act.wait_ge(mT_ok, h)
                elif kind == "tail":
                    act.wait_ge(mT_ok, 4)
                for i in range(2):
                    act.wait_ge(w_used, tile_done(h, 3, i))
                    A(sigo[:, i, :], ps[2 + i][:], ACT.Sigmoid if kind == "head" else ACT.Copy).then_inc(proj_sb, 1)

            def exps(m, i, base):
                act.wait_ge(md_ok, base + i + 1)
                if i:
                    act.wait_ge(p_ok, base + i)
                for j in range(i + 1):
                    col = PAIR[(i, j)] * GR
                    A(Et[:, j, :], md[:, 0, :] if j == i else bc[:, 0, i * P:(i + 1) * P], ACT.Exp, scale=-1.0,
                      bias=acol[:, bass.ds(m + col, 1)])
                for j in range(i, TB):
                    col = PAIR[(3 - i, 3 - j)] * GR + 32
                    last = A(Et[:, j + 1, :], md[:, 1, :] if j == i else bc[:, 1, i * P:(i + 1) * P], ACT.Exp,
                             scale=-1.0, bias=acol[:, bass.ds(m + col, 1)])
                last.then_inc(e_ok, 1)

            def rot(k):
                if k >= 2:
                    act.wait_ge(rope_ok, k - 1)
                act.wait_ge(proj_sb, (33, 34, 35, 36, 39, 40, 41, 42, 43, 44)[k])
                R = Pt[:, k % 2, 0:4, :].rearrange("p a b -> p (a b)")
                A(R[0:64, :], ROPE[k][64:P, :], ACT.Copy)
                A(R[64:P, :], ROPE[k][0:64, :], ACT.Copy).then_inc(rot_ok, 1)

            def body(h, kind, steps=8):
                mixing = kind in ("head", "tail")
                m = h - 1
                for j in range(steps):
                    s2 = h * 8 + (3 + j)
                    if not isinstance(h, int) or s2 < NB:
                        act.wait_ge(w_used, h * 16 + (4 + 2 * j))
                        hi(s2, (3 + j) % 2, h * 4 + ((3 + j) // 2 + 1))
                    if j == 0 and kind != "first":
                        o_gate(m, "tail" if kind == "end" else "head")
                    if j == 0 and mixing:
                        for d in range(2):
                            act.wait_ge(bc_ps, h)
                            A(bc[:, d, :], ps[6 + d][:], ACT.Copy).then_inc(bc_sb, 1)
                    if j < 4 and mixing:
                        exps(m, j, m * 4)
                    if j == 0 and kind == "first":
                        gates()
                    if j == 5 and kind == "first":
                        exp_minus_m()
                    if j == 2:
                        if kind == "head":
                            act.wait_ge(conv_ok, h * 4)
                        for i in range(2):
                            evac(qk[:, i, :] if kind == "end" else convin[:, i, 2:2 + S], i, tile_done(h, 0, i))
                    if j == 4:
                        for i in range(2):
                            evac(convin[:, 2 + i, 2:2 + S], 2 + i, tile_done(h, 1, i))
                    if kind in ("first", "head") and j in (5, 6):
                        for i in range(2):
                            t = 2 * (j - 5) + i
                            act.wait_ge(conv_pre, h * 4 + (t + 1))
                            A(Pt[:, i, 0:4, :].rearrange("p a b -> p (a b)"), qk[:, t, :], ACT.Sigmoid)\
                                .then_inc(conv_sig, 1)
                    if kind == "tail" and j in (5, 6):
                        if j == 5:
                            act.wait_ge(num_ps, 16)
                        rot(2 * (j - 5))
                        rot(2 * (j - 5) + 1)
                    if j == 6:
                        if mixing:
                            act.wait_ge(ht_ps, h)
                        for i in range(2):
                            evac(vT[:, i, :], i, tile_done(h, 2, i))
                    if j == 7:
                        act.wait_ge(vtr_ps, h + 1)
                        for i in range(2):
                            A(V[:, 2 * i:2 * i + 2, 0:HD], ps[4 + i][:].rearrange("p (c e) -> p c e", c=2),
                              ACT.Copy).then_inc(v_ok, 1)
                    if kind == "end" and j in (1, 3):
                        rot(j + 3)
                        rot(j + 4)

            body(0, "first")
            with act.Fori(1, HEADS) as h:
                body(h, "head")
            body(4, "tail")
            body(5, "end", steps=4)
            for i in range(2):
                evac(qk[:, 2 + i, :], 2 + i, tile_done(5, 1, i))
            rot(8)
            rot(9)
            act.wait_ge(w_used, 2 * NB)
            for g in range(2):
                A(o_hi[:, 4 * g:4 * g + 4, :], mT[:, 4 * g:4 * g + 4, :], ACT.Copy).then_inc(mhi_ok, 1)

            def vhi(v, par, cnt, base=None):
                act.wait_ge(v_ld[par], cnt)
                A(whi[par][:], wraw[par][:], ACT.Copy).then_inc(vhi_ok, 1)

            vhi(0, 0, 16)
            vhi(1, 1, 16)
            def pt_copy(u):
                n, _ = UNITS[u]
                w = len(blocks(n)) * P
                act.wait_ge(pt_ps, u + 1)
                if u >= 2:
                    act.wait_ge(pv_ps, u - 1)
                A(prT[:, u % 2, 0:w], ps[2 + u % 2][:, 0:w], ACT.Copy).then_inc(pt_sb, 1)

            for u, (n, hh) in enumerate(UNITS):
                w = len(blocks(n)) * P
                act.wait_ge(nm_ok, u + 1)
                if u >= 2:
                    act.wait_ge(pt_ps, u - 1)
                A(pr[:, u % 2, 0:w], sc[:, u % 2, 0:w], ACT.Exp, scale=-1.0, bias=sm[:, u, 0:1],
                  accum_out=sm[:, u, 1:2]).then_inc(ex_ok, 1)
                A(sm[:, u, 2:3], sinkb[:, hh:hh + 1], ACT.Exp, bias=sm[:, u, 0:1]).then_inc(es_ok, 1)
                if u >= 1:
                    pt_copy(u - 1)
            pt_copy(31)
            for n in range(TB):
                act.wait_ge(ao_ok, 29 + n)
                if n:
                    act.wait_ge(assq_ok, n)
                A(ajunk[:], aout[:, n, :], ACT.Square, accum_out=ssq[:, n:n + 1]).then_inc(assq_ok, 1)
            for k in range(8):
                act.wait_ge(at_ps, k + 1)
                A(o_hi[:, 8 + k, :], ps[k][:], ACT.Copy, scale=cols[:, C_GA + k:C_GA + k + 1]).then_inc(ohi_ok, 1)

            def squares(n0, n, ready, count):
                act.wait_ge(ready, count)
                if n >= 2:
                    act.wait_ge(ssum_ok, n0 + n - 1)
                A(sqt[:, n % 2, :], xT[:, n, :], ACT.Square).then_inc(sq_ok, 1)

            for v in range(NC_):
                act.wait_ge(v_used, 4 * v + 4)
                vhi(v + 2, v % 2, 16 * (v // 2 + 2))
                if v % 4 == 2 and v >= 4:
                    for i in range(4):
                        squares(0, 4 * (v // 4 - 1) + i, c_add, 4 * (v // 4 - 1) + i + 1)
            for i in range(4):
                squares(0, 12 + i, c_add, 13 + i)
            for kt in range(KT):
                act.wait_ge(n_mul, kt + 1)
                A(f_hi[:, kt, :], ht[:, kt % 2, :], ACT.Identity, scale=mod[:, 4, kt:kt + 1],
                  bias=mod[:, 3, kt:kt + 1]).then_inc(fhi_ok, 1)

            def split_step(vb, k):
                act.wait_ge(v_used, vb * 4 + (4 * k + 4))
                par = k % 2
                act.wait_ge(v_ld[par], vb * 8 + 16 * (k // 2 + 2))
                A(whi[par][:], wraw[par][:], ACT.Copy).then_inc(vhi_ok, 1)

            def g_unit(v4, c4):
                for i in range(4):
                    act.wait_ge(v_used, v4 + (i + 1))
                    if isinstance(c4, int) and c4 == 0:
                        pass
                    else:
                        act.wait_ge(alo_ok, c4 + (i - 3))
                    A(gs[:, i, :], ps[i][:], ACT.Sigmoid).then_inc(sig_ok, 1)

            def u_unit(uu):
                for i in range(4):
                    act.wait_ge(f_free, uu * 4 + (i + 1))
                    A(a_hi[:, i, :], gs[:, i, :], ACT.Copy).then_inc(ahi_ok, 1)

            for k in range(8):
                if k == 3:
                    g_unit(4 * 19, 0)
                if k == 7:
                    u_unit(1)
                split_step(16, k)
            with act.Fori(0, NCH - 1) as i:
                for k in range(12):
                    if k == 3:
                        g_unit(i * 48 + 4 * 27, i * 4 + 4)
                    if k == 11:
                        u_unit(i * 6 + 7)
                    split_step(i * 12 + 24, k)
            for k in range(4):
                if k < 2:
                    split_step(144, k)
                for i in range(4):
                    squares(KT, 4 * k + i, f_free, 4 * 62 + 4 * k + i + 1)
            act.wait_ge(n_rs, 2)
            act.wait_ge(y_sb, KT)
            for tb in range(2, TB):
                A(yout[:, tb, :], yout[:, tb, :], ACT.Copy, scale=rs[:, tb:tb + 1]).then_inc(y_okb, 1)

        @block.vector
        def _(dve):
            V_ = nc.vector
            ch = Chain(dve, dve_chain)
            dve.wait_ge(cst_T, 1)
            V_.tensor_copy(cols[:, 0:C_WC + 80], ps[7][:, 0:C_END]).then_inc(cst_ok, 1)
            dve.wait_ge(silu_sig, 1)
            dve.wait_ge(cst_ok, 1)
            V_.tensor_tensor(csil[:], cols[:, C_C:C_C + 16], tiny[:, 40:56], ALU.mult).then_inc(silu_ok, 1)
            dve.wait_ge(silu_ok, 1)

            def ada_op(n, slot, ld, cnt, kt, first):
                dve.wait_ge(ada_ld[ld], cnt)
                if first:
                    V_.tensor_scalar(acc[:], slot[:], csil[:, kt:kt + 1], None, ALU.mult).then_inc(ada_acc, 1)
                else:
                    dve.wait_ge(ada_acc, n)
                    V_.scalar_tensor_tensor(out=acc[:], in0=slot[:], scalar=csil[:, kt:kt + 1], in1=acc[:],
                                            op0=ALU.mult, op1=ALU.add).then_inc(ada_acc, 1)

            def ada_take(n, which, bank):
                dve.wait_ge(ada_sum, n + 1)
                j = 4 * (n % 4) if isinstance(n, int) else None
                V_.tensor_reduce(modp[:, which, j:j + 4], ps[bank][:].rearrange("p (a b) -> p a b", a=4), AX.X, ALU.add)\
                    .then_inc(modp_ok, 1)

            def mean_square(tb):
                dve.wait_ge(ssq_ok, tb + 1)
                V_.tensor_scalar(rsx[:, tb:tb + 1], ssq[:, tb:tb + 1], 1.0 / D, EPS, ALU.mult, ALU.add)\
                    .then_inc(ms_ok, 1)

            def normalise(tb):
                dve.wait_ge(rsx_ok, tb + 1)
                V_.tensor_scalar(xst[tb % 2][:], xst[tb % 2][:], rsx[:, tb:tb + 1], None, ALU.mult)\
                    .then_inc(xn_ok, 1)

            def trig():
                dve.wait_ge(const_ld, 16 * 13)
                ch.link(V_.tensor_copy(ang[:], posi[:]))
                ch.link(V_.tensor_scalar(ang[:], ang[:], invf[:, 0:1], None, ALU.mult))

            def trig_round(scale):
                ch.link(V_.tensor_scalar(kf[:], ang[:], 1.0 / (TWO_PI * scale), MAGIC, ALU.mult, ALU.add))
                ch.link(V_.tensor_scalar(kf[:], kf[:], -MAGIC, None, ALU.add))
                for part in (PI_1, PI_2, PI_3):
                    ch.link(V_.scalar_tensor_tensor(out=ang[:], in0=kf[:], scalar=-part * scale, in1=ang[:],
                                                    op0=ALU.mult, op1=ALU.add))

            def trig_end():
                V_.tensor_scalar(ang[:], ang[:], PI_SAFE, -PI_SAFE, ALU.min, ALU.max).then_inc(trig_in, 1)

            ring0 = [wraw[0], wraw[1], araw[0], araw[1]]
            n = 0
            for hidx, (q, half) in enumerate(HALF0):
                for j in range(8):
                    ada_op(n, ring0[n % 4], n % 4, 16 * (n // 4 + 1), 8 * half + j, j == 0)
                    n += 1
                    if n % 4 == 3 and n // 4 < TB:
                        mean_square(n // 4)
                    if n % 4 == 1 and 1 <= n // 4 <= TB:
                        normalise(n // 4 - 1)
                    if n == 2:
                        trig()
                    if n == 3:
                        trig_round(2048.0)
                    if n == 4:
                        trig_round(1.0)
                        trig_end()
                for b in range(4):
                    ada_take(4 * hidx + b, q + 6 * half, 4 + b)
            dve.wait_ge(modp_ok, 16)

            def add_bias(q):
                ch.link(V_.tensor_tensor(mod[:, q, :], modp[:, q, :], modp[:, q + 6, :], ALU.add))
                ch.link(V_.tensor_tensor(mod[:, q, :], mod[:, q, :], cols[:, C_BA + 16 * q:C_BA + 16 * q + 16], ALU.add))

            def scale_gain(q, g):
                return (V_.scalar_tensor_tensor(out=mod[:, q, :], in0=mod[:, q, :], scalar=1.0,
                                                in1=cols[:, g:g + 16], op0=ALU.add, op1=ALU.mult))

            add_bias(0)
            add_bias(1)
            scale_gain(1, C_G1).then_inc(mod_ok, 1)
            dve.wait_ge(mod_ok, 1)
            dve.wait_ge(xT_sb, 16)
            for kt in range(KT):
                if kt >= 2:
                    dve.wait_ge(hlo_ok, kt - 1)
                ch.link(V_.tensor_scalar(hf[:, kt % 2, :], xnT[:, kt, :], mod[:, 1, kt:kt + 1],
                                         mod[:, 0, kt:kt + 1], ALU.mult, ALU.add))
                dve.wait_ge(hhi_ok, kt + 1)
                V_.tensor_tensor(h_lo[:, kt, :], hf[:, kt % 2, :], h_hi[:, kt, :].bitcast(F32), ALU.subtract)\
                    .then_inc(hlo_ok, 1)

            ch.link(V_.memset(convin[:, :, 0:2], 0.0))
            ch.link(V_.memset(convin[:, :, S + 2:S + 4], 0.0))
            ch.link(V_.memset(V[:, :, HD:HD + 1], 1.0))
            ch.link(V_.memset(selI[:], 0.0))
            ch.link(V_.memset(selZ[:], 0.0))
            for dst, src in ((selI[:, 0:4], 0), (selI[:, 32:36], 8), (selZ[:, 0:4], 4), (selZ[:, 32:36], 12)):
                ch.link(V_.tensor_copy(dst, ident[0:GATES, src:src + 4]))

            def gates_in():
                dve.wait_ge(w_used, 2)
                V_.tensor_scalar(gsb[:], ps[4][0:GATES, :], bgate[:, 0:1], None, ALU.add).then_inc(gate_sb, 1)

            def gate_rows_():
                dve.wait_ge(gate_sel, 1)
                for dst, bank in ((li, 5), (zz, 6)):
                    ch.link(V_.tensor_copy(dst[0:32, :], ps[bank][0:32, :]))
                    ch.link(V_.tensor_copy(dst[32:64, :], ps[bank][32:64, ::-1]))
                V_.scalar_tensor_tensor(out=az[:], in0=zz[:], scalar=-1.0, in1=zz[:], op0=ALU.mult, op1=ALU.max)\
                    .then_inc(gate_rows, 1)
                dve.wait_ge(gate_rows, 1)
                ch.link(V_.tensor_scalar(zz[:], zz[:], 0.0, None, ALU.min))
                ch.link(V_.memset(blm[:, 0:1], 0.0))
                dve.wait_ge(gate_ln, 1)
                ch.link(V_.tensor_tensor(zz[:], zz[:], az[:], ALU.add))

                def chunk(j):
                    return slice(j * P, (j + 1) * P)

                for j in range(TB):
                    ch.link(V_.tensor_tensor_scan(bb[:, chunk(j)], ones[0:64, :], zz[:, chunk(j)], 0.0,
                                                  ALU.mult, ALU.add))
                ch.link(V_.tensor_tensor(aa[:], li[:], bb[:], ALU.subtract))
                for j in range(TB):
                    ch.link(V_.tensor_tensor_scan(mx[:, chunk(j)], aa[:, chunk(j)], aa[:, chunk(j)],
                                                  blm[:, j:j + 1], ALU.max, ALU.max))
                    e = (j + 1) * P - 1
                    ch.link(V_.tensor_tensor(blm[:, j + 1:j + 2], bb[:, e:e + 1], mx[:, e:e + 1], ALU.add))
                ch.link(V_.tensor_copy(mnat[0:32, :], mx[0:32, :]))
                ch.link(V_.tensor_copy(mnat[32:64, :], mx[32:64, ::-1]))
                ch.link(V_.tensor_tensor(az[0:32, :], bb[0:32, :], mx[0:32, :], ALU.add))
                ch.link(V_.tensor_tensor(az[32:64, :], bb[32:64, ::-1], mx[32:64, ::-1], ALU.add))
                for j in range(TB):
                    for i in range(j, TB):
                        k = PAIR[(i, j)]
                        bl = bb[:, i * P - 1:i * P] if i else None
                        off = blm[:, 8:9]
                        if i == j + 1:
                            ch.link(V_.tensor_copy(off, bl))
                        elif i > j:
                            ch.link(V_.tensor_tensor(off, off, bl, ALU.add))
                        back = aa[32:64, chunk(j)][:, ::-1]
                        if i == j:
                            ch.link(V_.tensor_copy(arow[0:32, k, :], aa[0:32, chunk(j)]))
                            ch.link(V_.tensor_copy(arow[32:64, k, :], back))
                        else:
                            ch.link(V_.tensor_scalar(arow[0:32, k, :], aa[0:32, chunk(j)], off[0:32], None, ALU.add))
                            ch.link(V_.tensor_scalar(arow[32:64, k, :], back, off[32:64], None, ALU.add))
                V_.tensor_copy(arow[0:1, 0, 0:1], arow[0:1, 0, 0:1]).then_inc(arow_ok, 1)
            def gate_columns():
                dve.wait_ge(gcol_ps, 1)
                V_.tensor_copy(acol[:], ps[7][:, 0:14 * GR]).then_inc(gcol_sb, 1)

            def select(h):
                if not (isinstance(h, int) and h == 0):
                    dve.wait_ge(bc_ps, h)
                for d in range(2):
                    last = V_.tensor_copy(sel2[:, d, :], ident[0:64, bass.ds(h + 32 * d, 1)].to_broadcast([64, P]))
                last.then_inc(sel_ok, 1)

            def diag(m, j):
                if j == 0:
                    dve.wait_ge(bc_sb, m * 2 + 2)
                if j:
                    dve.wait_ge(e_ok, m * 4 + j)
                V_.tensor_tensor(md[:, 0, :], bc[:, 0, j * P:(j + 1) * P], mask_up, ALU.subtract)
                V_.tensor_tensor(md[:, 1, :], bc[:, 1, j * P:(j + 1) * P], mask_lo, ALU.subtract).then_inc(md_ok, 1)

            def weigh(m, j):
                dve.wait_ge(s_ps, m * 4 + (j + 1))
                dve.wait_ge(e_ok, m * 4 + (j + 1))
                if j >= 2:
                    dve.wait_ge(num_ps, m * 4 + (j - 1))
                S3 = ps[4][:].rearrange("p (c t) -> p c t", c=TB)
                V_.tensor_tensor(Pt[:, j % 2, 0:j + 1, :], S3[:, 0:j + 1, :], Et[:, 0:j + 1, :], ALU.mult)
                V_.tensor_tensor(Pt[:, j % 2, j + 1:5, :], S3[:, j:TB, :], Et[:, j + 1:5, :], ALU.mult)\
                    .then_inc(p_ok, 1)

            def combine(m, j):
                if isinstance(m, int) and m == 0 and j == 0:
                    dve.wait_ge(em_ok, 1)
                dve.wait_ge(num_ps, m * 4 + (j + 1))
                for d in range(2):
                    den = ps[6 + d][:, HD:HD + 1]
                    ch.link(V_.tensor_scalar(dd[:, d:d + 1], den, -1.0,
                                             acol[:, bass.ds(m + ((10 + j) * GR + 32 * d), 1)], ALU.mult, ALU.max))
                    ch.link(V_.tensor_tensor(dd[:, d:d + 1], dd[:, d:d + 1], den, ALU.max))
                ch.link(V_.reciprocal(rr, dd))
                ch.link(V_.tensor_scalar(hm[:, j, :], ps[6][:, 0:HD], rr[:, 0:1], None, ALU.mult))
                V_.scalar_tensor_tensor(out=hm[:, j, :], in0=ps[7][:, 0:HD], scalar=rr[:, 1:2], in1=hm[:, j, :],
                                        op0=ALU.mult, op1=ALU.add).then_inc(num_used, 1)
                dve.wait_ge(num_used, m * 4 + (j + 1))
                ch.link(V_.bn_stats(st6, hm[:, j, :]))
                V_.tensor_copy(tiny[:, 56:57], rr[:, 0:1])
                ch.link(V_.bn_aggr(mv[:, 2 * j:2 * j + 2], st6))
                if j == TB - 1:
                    V_.tensor_scalar(ve, mv.rearrange("p (c k) -> p c k", k=2)[:, :, 1], EPS, None, ALU.add)\
                        .then_inc(var_ok, 1)

            def layer_norm(m):
                dve.wait_ge(rs_ok, m + 1)
                for j in range(TB):
                    last = V_.tensor_scalar(hm[:, j, :], hm[:, j, :], mv[:, 2 * j:2 * j + 1], rs[:, j:j + 1],
                                            ALU.subtract, ALU.mult)
                last.then_inc(hn_ok, 1)

            def mlstm_out(m):
                dve.wait_ge(ht_ps, m + 1)
                dve.wait_ge(proj_sb, m * 8 + 8)
                for d in range(2):
                    last = V_.scalar_tensor_tensor(
                        out=mT[:, bass.ds(m * 2 + d, 1), :].rearrange("p a t -> p (a t)"), in0=ps[4 + d][:],
                        scalar=cols[:, bass.ds(m * 2 + (C_GM + d), 1)], in1=sigo[:, d, :], op0=ALU.mult, op1=ALU.mult)
                last.then_inc(mT_ok, 1)

            def conv(h, t):
                dve.wait_ge(proj_sb, h * 8 + (2 if t < 2 else 4))
                tile = h * 2 + (t if t < 2 else 6 + t)
                ch.link(V_.tensor_scalar(qk[:, t, :], convin[:, t, 0:S], cols[:, bass.ds(tile + C_WC, 1)],
                                         cols[:, bass.ds(tile + C_BC, 1)], ALU.mult, ALU.add))
                for k in range(1, CONV):
                    ins = V_.scalar_tensor_tensor(out=qk[:, t, :], in0=convin[:, t, k:k + S],
                                                  scalar=cols[:, bass.ds(tile + (C_WC + 16 * k), 1)],
                                                  in1=qk[:, t, :], op0=ALU.mult, op1=ALU.add)
                    if k < CONV - 1:
                        ch.link(ins)
                ins.then_inc(conv_pre, 1)

            def silu(h, t):
                dve.wait_ge(conv_sig, h * 4 + (t + 1))
                V_.scalar_tensor_tensor(out=qk[:, t, :], in0=qk[:, t, :], scalar=1.0 if t < 2 else HD ** -0.5,
                                        in1=Pt[:, t % 2, 0:4, :].rearrange("p a b -> p (a b)"),
                                        op0=ALU.mult, op1=ALU.mult).then_inc(conv_ok, 1)

            def rope(k):
                dve.wait_ge(rot_ok, k + 1)
                if k == 0:
                    dve.wait_ge(trig_ok, 3)
                R = Pt[:, k % 2, 0:4, :].rearrange("p a b -> p (a b)")
                ch.link(V_.tensor_tensor(ROPE[k], ROPE[k], cosT[:], ALU.mult))
                ch.link(V_.tensor_tensor(R, R, sinT[:], ALU.mult))
                V_.tensor_tensor(ROPE[k], ROPE[k], R, ALU.add).then_inc(rope_ok, 1)

            def ada_b(par, m_base, j, kt, first, cnt):
                dve.wait_ge(ada_ld[2 + par], cnt)
                if first:
                    V_.tensor_scalar(acc[:], araw[par][:], csil[:, kt:kt + 1], None, ALU.mult).then_inc(ada_acc, 1)
                else:
                    dve.wait_ge(ada_acc, m_base + (32 + j))
                    V_.scalar_tensor_tensor(out=acc[:], in0=araw[par][:], scalar=csil[:, kt:kt + 1], in1=acc[:],
                                            op0=ALU.mult, op1=ALU.add).then_inc(ada_acc, 1)

            def body(h, kind, steps=8):
                mixing = kind in ("head", "tail")
                m = h - 1
                for j in range(steps):
                    for i in (range(2 * j, 2 * j + 2) if kind == "end" else
                              {0: (), 1: (0, 1), 2: (2,), 3: (3,), 4: (4, 5), 5: (6, 7)}.get(j, ())):
                        if kind == "end":
                            ada_b(i % 2, 40, i, 8 + i, i == 0, 16 * (8 + 20 + i // 2 + 1))
                        else:
                            ada_b(i % 2, h * 8, i, i if kind != "tail" else 8 + i, i == 0,
                                  h * 64 + 16 * (8 + i // 2 + 1))
                    if kind == "first" and j == 0:
                        gates_in()
                        gate_rows_()
                    if kind == "first" and j == 5:
                        gate_columns()
                    if mixing and j < 4:
                        diag(m, j)
                    if mixing and 1 <= j <= 4:
                        combine(m, j - 1)
                    if mixing and j < 4:
                        weigh(m, j)
                    if mixing and j == 5:
                        layer_norm(m)
                    if mixing and j == 6:
                        mlstm_out(m)
                    if kind in ("first", "head") and j in (5, 6):
                        t = 2 * (j - 5)
                        conv(h, t)
                        conv(h, t + 1)
                        silu(h, t)
                        silu(h, t + 1)
                    if kind == "tail" and j in (5, 6):
                        rope(2 * (j - 5))
                        rope(2 * (j - 5) + 1)
                    if kind == "end" and j in (1, 3):
                        rope(j + 3)
                        rope(j + 4)
                    if kind in ("first", "head") and j == 7:
                        select(h)
                    if kind != "end" and j in (6, 7):
                        which = h + 2 if kind != "tail" else 2 + 6
                        for b in range(2):
                            dve.wait_ge(ada_sum, h * 4 + (17 + 2 * (j - 6) + b))
                            q = 4 * (2 * (j - 6) + b)
                            V_.tensor_reduce(modp[:, bass.ds(which, 1), q:q + 4].rearrange("p a k -> p (a k)"),
                                             ps[6 + b][:].rearrange("p (a b) -> p a b", a=4), AX.X, ALU.add)\
                                .then_inc(modp_ok, 1)
                if kind == "end":
                    for b in range(4):
                        ada_take(36 + b, 3 + 6, 4 + b)

            body(0, "first")
            LINKS = 8 * TB + 4 * 4
            with dve.Fori(1, HEADS) as h:
                ch.enter(h, 1, LINKS)
                body(h, "head")
            ch.leave(HEADS - 1)
            body(4, "tail")
            body(5, "end", steps=4)
            dve.wait_ge(w_used, 2 * NB)
            for g in range(2):
                dve.wait_ge(mhi_ok, g + 1)
                V_.tensor_tensor(o_lo[:, 4 * g:4 * g + 4, :], mT[:, 4 * g:4 * g + 4, :],
                                 o_hi[:, 4 * g:4 * g + 4, :].bitcast(F32), ALU.subtract).then_inc(mlo_ok, 1)
            rope(8)
            rope(9)
            dve.wait_ge(modp_ok, 40)
            add_bias(2)
            ch.link(V_.tensor_scalar(nsink[:], sinkb[:], -1.0, None, ALU.mult))

            def vlo(v_hi, par):
                dve.wait_ge(vhi_ok, v_hi)
                V_.tensor_tensor(wlo[par][:], wraw[par][:], whi[par][:].bitcast(F32), ALU.subtract)\
                    .then_inc(vlo_ok, 1)

            vlo(1, 0)
            vlo(2, 1)
            dve.wait_ge(mlo_ok, 2)

            def softmax_in(u):
                n, hh = UNITS[u]
                bl = blocks(n)
                w = len(bl) * P
                m0 = (bl[0] - n + 1) * P
                dve.wait_ge(as_ps, u + 1)
                if u >= 2:
                    dve.wait_ge(ex_ok, u - 1)
                V_.tensor_tensor_reduce(out=sc[:, u % 2, 0:w], in0=ps[u % 2][:, 0:w], in1=mask3[:, m0:m0 + w],
                                        scale=-AD ** -0.5, scalar=nsink[:, hh:hh + 1], op0=ALU.add, op1=ALU.min,
                                        accum_out=sm[:, u, 0:1]).then_inc(nm_ok, 1)

            def head_out(u):
                n, hh = UNITS[u]
                dve.wait_ge(es_ok, u + 1)
                ch.link(V_.tensor_tensor(sm[:, u, 3:4], sm[:, u, 1:2], sm[:, u, 2:3], ALU.add))
                ch.link(V_.reciprocal(sm[:, u, 3:4], sm[:, u, 3:4]))
                dve.wait_ge(pv_ps, u + 1)
                V_.tensor_scalar(aout[:, n, hh * AD:(hh + 1) * AD], ps[4 + u % 2][:, 0:AD], sm[:, u, 3:4], None,
                                 ALU.mult).then_inc(ao_ok, 1)

            for u in range(32):
                softmax_in(u)
                if u >= 2:
                    head_out(u - 2)
            head_out(30)
            head_out(31)
            dve.wait_ge(assq_ok, TB)
            V_.tensor_scalar(ve, ssq, 1.0 / (AH * AD), EPS, ALU.mult, ALU.add).then_inc(ams_ok, 1)
            dve.wait_ge(ars_ok, 1)
            for n in range(TB):
                V_.tensor_scalar(aout[:, n, :], aout[:, n, :], rs[:, n:n + 1], None, ALU.mult).then_inc(aon_ok, 1)
            for k in range(8):
                dve.wait_ge(ohi_ok, k + 1)
                V_.scalar_tensor_tensor(out=o_lo[:, 8 + k, :], in0=ps[k][:], scalar=cols[:, C_GA + k:C_GA + k + 1],
                                        in1=o_hi[:, 8 + k, :].bitcast(F32), op0=ALU.mult, op1=ALU.subtract)\
                    .then_inc(olo_ok, 1)

            def add_x(u):
                dve.wait_ge(ct_ps, u + 1)
                for i in range(4):
                    V_.tensor_tensor(xT[:, 4 * u + i, :], xT[:, 4 * u + i, :], ps[4 * (u % 2) + i][:], ALU.add)\
                        .then_inc(c_add, 1)

            for v in range(NC_):
                u = v // 4
                ada_b(v % 2, 48, v, 8 + v % 8, v % 8 == 0, 16 * (8 + 24 + v // 2 + 1))
                if v == 7:
                    for b in range(4):
                        ada_take(40 + b, 4 + 6, b)
                if v % 4 == 2 and v >= 4:
                    add_x(u - 1)
                if v % 4 == 3:
                    for i in range(4):
                        dve.wait_ge(v_used, 4 * v + i + 1)
                        V_.tensor_scalar(xT[:, 4 * u + i, :], ps[4 * (u % 2) + i][:], mod[:, 2, 4 * u + i:4 * u + i + 1],
                                         None, ALU.mult).then_inc(c_sb, 1)
                vlo(v + 3, v % 2)
            dve.wait_ge(c_sb, 16)
            add_x(3)
            for b in range(4):
                ada_take(44 + b, 5 + 6, b)
            dve.wait_ge(modp_ok, 48)
            for q in (3, 4, 5):
                add_bias(q)
            ch.link(scale_gain(4, C_G2))

            def inv_rms():
                V_.tensor_scalar(ve, ps[6][:, 0:4], 1.0 / D, EPS, ALU.mult, ALU.add).then_inc(n_ms, 1)

            dve.wait_ge(n_ps, 1)
            inv_rms()
            dve.wait_ge(n_rs, 1)
            for tb in range(TB):
                last = V_.tensor_scalar(sqt[:, 0, tb * P:(tb + 1) * P], ident[:], rs[:, tb:tb + 1], None, ALU.mult)
            last.then_inc(n_dg, 1)
            dve.wait_ge(n_bc, 1)
            for kt in range(KT):
                if kt >= 2:
                    dve.wait_ge(fhi_ok, kt - 1)
                V_.tensor_tensor(ht[:, kt % 2, :], xT[:, kt, :], ps[7][:], ALU.mult).then_inc(n_mul, 1)
                dve.wait_ge(n_mul, kt + 1)
                ch.link(V_.tensor_scalar(hu[:, kt % 2, :], ht[:, kt % 2, :], mod[:, 4, kt:kt + 1],
                                         mod[:, 3, kt:kt + 1], ALU.mult, ALU.add))
                dve.wait_ge(fhi_ok, kt + 1)
                V_.tensor_tensor(f_lo[:, kt, :], hu[:, kt % 2, :], f_hi[:, kt, :].bitcast(F32), ALU.subtract)\
                    .then_inc(flo_ok, 1)

            def g_unit(c4):
                for i in range(4):
                    dve.wait_ge(sig_ok, c4 + (i + 1))
                    V_.tensor_tensor(gs[:, i, :], ps[i][:], gs[:, i, :], ALU.mult).then_inc(f_free, 1)

            def u_unit(v4, uu, c4):
                dve.wait_ge(f_free, uu * 4)
                for i in range(4):
                    dve.wait_ge(v_used, v4 + (i + 1))
                    V_.tensor_tensor(gs[:, i, :], ps[4 + i][:], gs[:, i, :], ALU.mult).then_inc(f_free, 1)
                    dve.wait_ge(ahi_ok, c4 + (i + 1))
                    V_.tensor_tensor(a_lo[:, i, :], gs[:, i, :], a_hi[:, i, :].bitcast(F32), ALU.subtract)\
                        .then_inc(alo_ok, 1)

            def d_tile(v4, u, bank, i):
                t = 4 * u + i
                dve.wait_ge(v_used, v4 + (i + 1))
                V_.scalar_tensor_tensor(out=xT[:, t, :], in0=ps[bank + i][:], scalar=mod[:, 5, t:t + 1],
                                        in1=xT[:, t, :], op0=ALU.mult, op1=ALU.add).then_inc(f_free, 1)

            def split_step(vb, k):
                dve.wait_ge(vhi_ok, vb + (k + 3))
                V_.tensor_tensor(wlo[k % 2][:], wraw[k % 2][:], whi[k % 2][:].bitcast(F32), ALU.subtract)\
                    .then_inc(vlo_ok, 1)

            for k in range(8):
                if k == 3:
                    g_unit(0)
                if k == 7:
                    u_unit(4 * 23, 1, 0)
                split_step(16, k)
            with dve.Fori(0, NCH - 1) as i:
                for k in range(12):
                    if k == 3:
                        g_unit(i * 4 + 4)
                    if 4 <= k < 8:
                        if k == 4:
                            dve.wait_ge(f_free, i * 24 + 12)
                        for t in range(4):
                            d_tile(i * 48 + 4 * (24 + k), k - 4, 4 * ((k + 1) % 2), t)
                    if k == 11:
                        u_unit(i * 48 + 4 * 35, i * 6 + 7, i * 4 + 4)
                    split_step(i * 12 + 24, k)
            dve.wait_ge(f_free, 4 * 62)

            def y_tile(u, i):
                t = 4 * u + i
                dve.wait_ge(yt_ps, 4 * u + i + 1)
                V_.tensor_tensor(yout[:, :, t * P:(t + 1) * P],
                                 ps[4 * (u % 2) + i][:].rearrange("p (b f) -> p b f", b=TB),
                                 gfb[:, t * P:(t + 1) * P].unsqueeze(1).to_broadcast([P, TB, P]), ALU.mult)\
                    .then_inc(y_sb, 1)

            for u in range(4):
                for i in range(4):
                    d_tile(4 * (144 + u), u, 4 * (u % 2), i)
                    if i == 1 and u:
                        if u == 1:
                            dve.wait_ge(gf_ld, 16)
                        for k in range(4):
                            y_tile(u - 1, k)
                if u < 2:
                    split_step(144, u)
            for k in range(4):
                y_tile(3, k)
            dve.wait_ge(n_ps, 2)
            inv_rms()
            dve.wait_ge(n_rs, 2)
            dve.wait_ge(y_sb, KT)
            for tb in range(2):
                V_.tensor_scalar(yout[:, tb, :], yout[:, tb, :], rs[:, tb:tb + 1], None, ALU.mult).then_inc(y_ok, 1)

        @block.tensor
        def _(pe):
            def mm3(o, w_hi, w_lo, m_hi, m_lo, first, last):
                pe.matmul(o, w_hi, m_hi, start=first, stop=False)
                pe.matmul(o, w_hi, m_lo, start=False, stop=False)
                return pe.matmul(o, w_lo, m_hi, start=False, stop=last)

            pe.wait_ge(const_ld, 16 * 13)
            pe.wait_ge(masks_ok, 5)
            for i, (n, off) in enumerate(((96, 0), (96, C_BA), (80, C_WC))):
                last = pe.transpose(ps[7][:, off:off + n], stg[0:n, i, :], ident[0:n, 0:n])
            last.then_inc(cst_T, 1)

            def x_block(tb):
                pe.wait_ge(xn_ok, tb + 1)
                for q in range(4):
                    if 4 * tb + q >= 2:
                        pe.wait_ge(xT_sb, 4 * tb + q - 1)
                    for i in range(4):
                        f = 4 * q + i
                        last = pe.transpose(ps[q % 2][:, i * P:(i + 1) * P], xst[tb % 2][:, f * P:(f + 1) * P], ident[:])
                    last.then_inc(xT_ps, 1)

            def ada_turn(hidx, banks, j0=0):
                if j0 == 0:
                    pe.wait_ge(ada_acc, hidx * 8 + 8)
                for b, bank in enumerate(banks):
                    for i in range(4):
                        j = 4 * (j0 + b) + i
                        last = pe.transpose(ps[bank][:, i * P:(i + 1) * P], acc[:, j * P:(j + 1) * P], ident[:])
                    last.then_inc(ada_sum, 1)

            pe.wait_ge(cst_ok, 1)
            x_block(0)
            ada_turn(0, (4, 5, 6, 7))
            x_block(1)
            x_block(2)
            pe.wait_ge(modp_ok, 4)
            ada_turn(1, (4, 5, 6, 7))
            x_block(3)
            pe.wait_ge(modp_ok, 8)
            ada_turn(2, (4, 5, 6, 7))
            pe.wait_ge(modp_ok, 12)
            ada_turn(3, (4, 5, 6, 7))

            def gate(kt):
                pe.wait_ge(hlo_ok, kt + 1)
                last = mm3(ps[4][:], w3(whi[0], 16)[:, kt, :], w3(wlo[0], 16)[:, kt, :], h_hi[:, kt, :], h_lo[:, kt, :],
                           kt == 0, kt == KT - 1)
                if kt in (7, 15):
                    last.then_inc(w_used, 1)

            def first_group(kt, done=False):
                for i in range(2):
                    last = mm3(ps[i][:], w3(whi[1], 8)[:, kt, i * P:(i + 1) * P], w3(wlo[1], 8)[:, kt, i * P:(i + 1) * P],
                               h_hi[:, kt, :], h_lo[:, kt, :], kt == 0, False)
                    if done:
                        last.then_inc(w_used, 1)

            pe.wait_ge(modp_ok, 16)
            pe.wait_ge(wlo_ok, 1)
            for kt in range(8):
                gate(kt)
                if kt == 1:
                    pe.wait_ge(wlo_ok, 2)
                if kt >= 1:
                    first_group(kt - 1)
            for kt in range(8, KT):
                gate(kt)
            first_group(7, done=True)

            def slot(h, j):
                par, g, kk = (1 + j) % 2, j // 2, j % 2
                pe.wait_ge(wlo_ok, h * 8 + (2 + j))
                for i in range(2):
                    bank = 2 * (g % 2) + i
                    if kk == 0 and not (isinstance(h, int) and 8 * h + 2 * g + i < 4):
                        pe.wait_ge(proj_sb, h * 8 + (2 * g + i - 3))
                    for k in range(8):
                        last = mm3(ps[bank][:], w3(whi[par], 8)[:, k, i * P:(i + 1) * P],
                                   w3(wlo[par], 8)[:, k, i * P:(i + 1) * P], h_hi[:, 8 * kk + k, :],
                                   h_lo[:, 8 * kk + k, :], kk == 0 and k == 0, kk == 1 and k == 7)
                    last.then_inc(w_used, 1)

            def gate_select():
                pe.wait_ge(gate_sb, 1)
                pe.matmul(ps[5][0:64, :], selI[:], gsb[:], start=True, stop=True)
                pe.matmul(ps[6][0:64, :], selZ[:], gsb[:], start=True, stop=True).then_inc(gate_sel, 1)

            def gate_columns():
                pe.wait_ge(arow_ok, 1)
                for k in range(14):
                    src = arow[:, k, :] if k < 10 else az[:, (k - 10) * P:(k - 9) * P]
                    last = pe.matmul(ps[7][:, k * GR:(k + 1) * GR], src, ident[0:64, 0:GR], start=True, stop=True)
                last.then_inc(gcol_ps, 1)

            def spread_m(m):
                pe.wait_ge(sel_ok, m + 1)
                pe.wait_ge(modp_ok, m * 4 + 20)
                for d in range(2):
                    last = pe.matmul(ps[6 + d][:], sel2[:, d, :], mnat[:], start=True, stop=True)
                last.then_inc(bc_ps, 1)

            def scores(m, i):
                if i == 0:
                    pe.wait_ge(conv_ok, m * 4 + 4)
                    pe.wait_ge(v_ok, m * 2 + 2)
                else:
                    pe.wait_ge(p_ok, m * 4 + i)
                for j in range(TB):
                    for d in range(2):
                        last = pe.matmul(ps[4][:, j * P:(j + 1) * P], qk[:, 2 + d, j * P:(j + 1) * P],
                                         qk[:, d, i * P:(i + 1) * P], start=(d == 0), stop=(d == 1))
                last.then_inc(s_ps, 1)

            def numerators(m, i):
                pe.wait_ge(p_ok, m * 4 + (i + 1))
                if i == 0:
                    pe.wait_ge(bc_sb, m * 2 + 2)
                else:
                    pe.wait_ge(num_used, m * 4 + i)
                for j in range(i + 1):
                    pe.matmul(ps[6][:, 0:HD + 1], Pt[:, i % 2, j, :], V[:, j, :], start=(j == 0), stop=(j == i))
                for j in range(i, TB):
                    last = pe.matmul(ps[7][:, 0:HD + 1], Pt[:, i % 2, j + 1, :], V[:, j, :], start=(j == i),
                                     stop=(j == TB - 1))
                last.then_inc(num_ps, 1)

            def turn_h(m):
                pe.wait_ge(hn_ok, m + 1)
                for d in range(2):
                    for i in range(TB):
                        last = pe.transpose(ps[4 + d][:, i * P:(i + 1) * P], hm[:, i, d * P:(d + 1) * P], ident[:])
                last.then_inc(ht_ps, 1)

            def turn_v(h, mixing):
                pe.wait_ge(proj_sb, h * 8 + 6)
                if mixing:
                    pe.wait_ge(mT_ok, h)
                for i in range(TB):
                    for d in range(2):
                        last = pe.transpose(ps[4 + i // 2][:, (i % 2) * HD + d * P:(i % 2) * HD + (d + 1) * P],
                                            vT[:, d, i * P:(i + 1) * P], ident[:])
                last.then_inc(vtr_ps, 1)

            def body(h, kind, steps=8):
                mixing = kind in ("head", "tail")
                m = h - 1
                for j in range(steps):
                    if not (kind == "first" and j == 0):
                        slot(h, j)
                    if kind == "first" and j == 0:
                        gate_select()
                    if kind == "first" and j == 4:
                        gate_columns()
                    if mixing and j == 0:
                        spread_m(m)
                    if mixing and 1 <= j <= 4:
                        numerators(m, j - 1)
                    if mixing and j < 4:
                        scores(m, j)
                    if j == 6:
                        if mixing:
                            pe.wait_ge(num_used, h * 4)
                            turn_h(m)
                        else:
                            pe.wait_ge(gcol_sb, 1)
                    if j == 6:
                        ada_turn(h + 4, (6, 7))
                    if j == 7:
                        pe.wait_ge(modp_ok, h * 4 + 18)
                        ada_turn(h + 4, (6, 7), 2)
                        turn_v(h, mixing)
                if kind == "end":
                    pe.wait_ge(modp_ok, 36)
                    pe.wait_ge(v_ok, 10)
                    ada_turn(9, (4, 5, 6, 7))

            body(0, "first")
            with pe.Fori(1, HEADS) as h:
                body(h, "head")
            body(4, "tail")
            body(5, "end", steps=4)

            def att_scores(u):
                n, hh = UNITS[u]
                pe.wait_ge(rope_ok, hh + 3)
                if u == 0:
                    pe.wait_ge(proj_sb, 44)
                if u >= 2:
                    pe.wait_ge(nm_ok, u - 1)
                bl = blocks(n)
                pe.matmul(ps[u % 2][:, 0:len(bl) * P], QH[hh][:, n * P:(n + 1) * P],
                          KG[hh // 4][:, bl[0] * P:(bl[-1] + 1) * P], start=True, stop=True).then_inc(as_ps, 1)

            def att_turn(u):
                n, hh = UNITS[u]
                pe.wait_ge(ex_ok, u + 1)
                if u >= 2:
                    pe.wait_ge(pt_sb, u - 1)
                for b in range(len(blocks(n))):
                    last = pe.transpose(ps[2 + u % 2][:, b * P:(b + 1) * P], pr[:, u % 2, b * P:(b + 1) * P], ident[:])
                last.then_inc(pt_ps, 1)

            def att_values(u):
                n, hh = UNITS[u]
                g = hh // 4
                bl = blocks(n)
                pe.wait_ge(pt_sb, u + 1)
                if u == 0:
                    pe.wait_ge(v_ok, 10)
                if u >= 2:
                    pe.wait_ge(ao_ok, u - 1)
                for b, k in enumerate(bl):
                    last = pe.matmul(ps[4 + u % 2][:, 0:AD], prT[:, u % 2, b * P:(b + 1) * P],
                                     V[:, k, g * AD:(g + 1) * AD], start=(b == 0), stop=(b == len(bl) - 1))
                last.then_inc(pv_ps, 1)

            att_scores(0)
            for u in range(32):
                if u + 1 < 32:
                    att_scores(u + 1)
                att_turn(u)
                if u >= 1:
                    att_values(u - 1)
            att_values(31)
            pe.wait_ge(ao_ok, 32)
            pe.wait_ge(aon_ok, TB)
            pe.wait_ge(modp_ok, 40)
            for k in range(8):
                for n in range(TB):
                    last = pe.transpose(ps[k][:, n * P:(n + 1) * P], aout[:, n, k * P:(k + 1) * P], ident[:])
                last.then_inc(at_ps, 1)

            def turn_x(u):
                pe.wait_ge(xs_ld[u % 2], 16 * (u // 2 + 1))
                pe.wait_ge(c_sb, 4 * (u + 1))
                for i in range(4):
                    for tb in range(TB):
                        last = pe.transpose(ps[4 * (u % 2) + i][:, tb * P:(tb + 1) * P],
                                            xs[u % 2][:, tb, i * P:(i + 1) * P], ident[:])
                last.then_inc(ct_ps, 1)

            def vslot(par, split, o, m_hi, m_lo, k0, first, last_, bank_free=None):
                pe.wait_ge(vlo_ok, split)
                for i in range(4):
                    if bank_free is not None:
                        pe.wait_ge(*bank_free(i))
                    for k in range(4):
                        last = mm3(ps[o + i][:], w3(whi[par], 4)[:, k, i * P:(i + 1) * P],
                                   w3(wlo[par], 4)[:, k, i * P:(i + 1) * P], m_hi[:, k0 + k, :], m_lo[:, k0 + k, :],
                                   first and k == 0, last_ and k == 3)
                    last.then_inc(v_used, 1)

            pe.wait_ge(mlo_ok, 2)
            for v in range(NC_):
                u, ks = v // 4, v % 4
                if ks == 2 and u == 0:
                    pe.wait_ge(olo_ok, 8)
                free = None
                if ks == 0 and u < 2:
                    free = lambda i, u=u: (olo_ok, 4 * u + i + 1)
                elif ks == 0:
                    free = lambda i, u=u: (c_add, 4 * (u - 2) + i + 1)
                    if u == 2:
                        pe.wait_ge(modp_ok, 44)
                vslot(v % 2, v + 1, 4 * (u % 2), o_hi, o_lo, 4 * ks, ks == 0, ks == 3, free)
                if ks == 1 and u:
                    turn_x(u - 1)
                if v == 7:
                    pe.wait_ge(c_add, 4)
                    ada_turn(10, (0, 1, 2, 3))
            pe.wait_ge(c_add, 12)
            turn_x(3)
            ada_turn(11, (0, 1, 2, 3))

            def sum_columns(k):
                pe.wait_ge(ssum_ok, KT * k)
                for tb in range(TB):
                    last = pe.matmul(ps[6][:, tb:tb + 1], ssum[:, tb * P:(tb + 1) * P], ones[:, 0:1], start=True, stop=True)
                last.then_inc(n_ps, 1)

            pe.wait_ge(c_add, 16)
            sum_columns(1)
            pe.wait_ge(n_dg, 1)
            for tb in range(TB):
                last = pe.matmul(ps[7][:, tb * P:(tb + 1) * P], ones[:], sqt[:, 0, tb * P:(tb + 1) * P], start=True, stop=True)
            last.then_inc(n_bc, 1)
            pe.wait_ge(modp_ok, 48)

            for ks in range(4):
                pe.wait_ge(vlo_ok, 17 + ks)
                for k in range(4):
                    pe.wait_ge(flo_ok, 4 * ks + k + 1)
                    for i in range(4):
                        last = mm3(ps[i][:], w3(whi[ks % 2], 4)[:, k, i * P:(i + 1) * P],
                                   w3(wlo[ks % 2], 4)[:, k, i * P:(i + 1) * P], f_hi[:, 4 * ks + k, :],
                                   f_lo[:, 4 * ks + k, :], ks == 0 and k == 0, ks == 3 and k == 3)
                        if k == 3:
                            last.then_inc(v_used, 1)
            for ks in range(4):
                vslot(ks % 2, 21 + ks, 4, f_hi, f_lo, 4 * ks, ks == 0, ks == 3)

            def unit_free(uu):
                return lambda i: (f_free, uu * 4 + (i - 7))

            with pe.Fori(0, NCH - 1) as i:
                for k in range(4):
                    vslot(k % 2, i * 12 + (25 + k), 0, f_hi, f_lo, 4 * k, k == 0, k == 3,
                          unit_free(i * 6 + 2) if k == 0 else None)
                pe.wait_ge(alo_ok, i * 4 + 4)
                for k in range(4, 8):
                    vslot(k % 2, i * 12 + (25 + k), 4 * ((k + 1) % 2), a_hi, a_lo, 0, True, True, unit_free(i * 6 + (k - 1)))
                for k in range(8, 12):
                    vslot(k % 2, i * 12 + (25 + k), 4, f_hi, f_lo, 4 * (k - 8), k == 8, k == 11,
                          unit_free(i * 6 + 7) if k == 8 else None)

            def turn_y(u):
                for i in range(4):
                    pe.wait_ge(f_free, 4 * 62 + 4 * u + i + 1)
                    for tb in range(TB):
                        last = pe.transpose(ps[4 * (u % 2) + i][:, tb * P:(tb + 1) * P],
                                            xT[:, 4 * u + i, tb * P:(tb + 1) * P], ident[:])
                    last.then_inc(yt_ps, 1)

            pe.wait_ge(alo_ok, 4 * NCH)
            for u in range(4):
                par = u % 2
                pe.wait_ge(vlo_ok, 145 + u)
                for i in range(4):
                    if u < 2:
                        pe.wait_ge(f_free, 4 * (60 + u) + i + 1)
                    else:
                        pe.wait_ge(y_sb, 4 * (u - 2) + i + 1)
                    for k in range(4):
                        last = mm3(ps[4 * (u % 2) + i][:], w3(whi[par], 4)[:, k, i * P:(i + 1) * P],
                                   w3(wlo[par], 4)[:, k, i * P:(i + 1) * P], a_hi[:, k, :], a_lo[:, k, :], k == 0, k == 3)
                    last.then_inc(v_used, 1)
                    if i == 1 and u:
                        turn_y(u - 1)
            turn_y(3)
            pe.wait_ge(y_sb, 12)
            pe.wait_ge(y_sb, 15)
            sum_columns(2)


_INS = ["x", "c", "positions", "w_ada", "b_ada", "g_norm1", "g_norm2", "w_in", "b_gates", "w_conv", "b_conv",
        "g_mlstm_out", "sink", "g_attn_out", "w_out", "w_gate", "w_up", "w_down", "g_final"]


def rope_constants():
    half = AD // 2
    inv = (10000.0 ** (-np.arange(half) * 2.0 / AD)).astype(np.float32)
    t = np.empty((P, 2), np.float32)
    t[:half, 0] = inv
    t[half:, 0] = inv
    t[:half, 1] = -1.0
    t[half:, 1] = 1.0
    return t


def kernel(**inputs):
    import concourse.bacc as _bacc
    from concourse.bass_utils import run_bass_kernel_spmd as _run

    nc = _bacc.Bacc("TRN2", target_bir_lowering=False, num_devices=1)
    arrays, args = {}, []
    for name in _INS:
        a = np.ascontiguousarray(inputs[name])
        arrays[f"in_{name}"] = a
        args.append(nc.dram_tensor(f"in_{name}", a.shape, mybir.dt.from_np(a.dtype), kind="ExternalInput").ap())
    t = rope_constants()
    arrays["rope_constants"] = t
    args.append(nc.dram_tensor("rope_constants", t.shape, F32, kind="ExternalInput").ap())
    args.append(nc.dram_tensor("out", (1, S, D), F32, kind="ExternalOutput").ap())
    program(nc, *args)
    r = _run(nc, [arrays], core_ids=[0])
    return r.results[0]["out"]
```

```python
from contextlib import ExitStack

import numpy as np
import concourse.bass as bass
from concourse import mybir

F32 = mybir.dt.float32
F32R = mybir.dt.float32r
I32 = mybir.dt.int32
ALU = mybir.AluOpType
ACT = mybir.ActivationFunctionType
AX = mybir.AxisListType

P = 128
D = 2048
S = 512
KT = D // P
TB = S // P
HEADS = 4
HD = 256
CONV = 5
AH = 8
AD = 128
GATES = 16
FF = 5632
CH = 512
NCH = FF // CH
SLOT = 2048
EPS = 1e-6
NEG = -1e30
MAGIC = 1.5 * 2.0 ** 23
TWO_PI = 2.0 * np.pi
PI_1 = 6.28125
PI_2 = float(np.round((TWO_PI - PI_1) * 2.0 ** 20) / 2.0 ** 20)
PI_3 = float(np.float32(TWO_PI - PI_1 - PI_2))
PI_SAFE = 3.1415925
COL_AK = 4 * 1024 + GATES + 1024
COL_AV = COL_AK + 256
COL_G = 4 * 1024
COL_AQ = COL_G + GATES

C_G1, C_G2, C_GF, C_BC, C_GM, C_GA, C_C, C_BA, C_WC, C_END = 0, 16, 32, 48, 64, 72, 80, 96, 192, 272

PAIRS = [(i, j) for i in range(TB) for j in range(i + 1)]
PAIR = {p: n for n, p in enumerate(PAIRS)}
GR = 36


class Chain:

    def __init__(self, eng, sem):
        self.eng, self.sem, self.base, self.n = eng, sem, 0, 0

    def link(self, ins):
        ins.then_inc(self.sem, 1)
        self.n += 1
        self.eng.wait_ge(self.sem, self.base + self.n)

    def enter(self, iteration, first, each):
        self.start, self.each = self.base + self.n, each
        self.base, self.n = iteration * each + (self.start - first * each), 0

    def leave(self, times):
        assert self.n == self.each, (self.n, self.each)
        self.base, self.n = self.start + self.each * times, 0


def program(nc, x, c, positions, w_ada, b_ada, g1, g2, w_in, b_gates, w_conv, b_conv, gm, sink, ga,
            w_out, w_gate, w_up, w_down, gf, rope_inv, out):
    ctx = ExitStack()
    with ctx:
        top = [16512]

        def at(name, shape, dt, off):
            return nc.alloc_sbuf_tensor_at(name, shape, dt, offset=off)

        def size(shape):
            n = 4
            for k in shape[1:]:
                n *= k
            return (n + 31) // 32 * 32

        def sb(name, shape, dt=F32):
            off = top[0]
            top[0] += size(shape)
            return at(name, shape, dt, off)

        def region(base, names):
            got, off = [], base
            for name, shape, dt in names:
                got.append(at(name, shape, dt, off))
                off += size(shape)
            return got, off

        ident = sb("ident", [P, P])
        mask3 = sb("mask3", [P, 3 * P])
        ones = sb("ones", [P, P])
        cols = sb("cols", [P, C_END])
        modp = sb("modp", [P, 12, KT])
        mod = sb("mod", [P, 6, KT])
        csil = sb("csil", [P, KT])
        acol = sb("acol", [P, 14 * GR])
        mnat = sb("mnat", [64, S])
        sel2 = sb("sel2", [64, 2, P])
        sinkb = sb("sinkb", [P, AH])
        nsink = sb("nsink", [P, AH])
        bgate = sb("bgate", [GATES, 1])
        invf = sb("invf", [P, 2])
        tiny = sb("tiny", [P, 64])
        cosT = sb("cosT", [P, S])
        sinT = sb("sinT", [P, S])
        mask_up, mask_lo = mask3[:, 0:P], mask3[:, 2 * P:3 * P]
        ssq, rsx, halfneg, dd, rr, mv, ve, rs, st6 = (
            tiny[:, 0:4], tiny[:, 4:8], tiny[:, 8:12], tiny[:, 12:14], tiny[:, 14:16], tiny[:, 16:24],
            tiny[:, 24:28], tiny[:, 28:32], tiny[:, 32:38])
        halfpi = tiny[:, 38:39]
        wraw = [sb(f"wraw{i}", [P, SLOT]) for i in range(2)]
        whi = [sb(f"whi{i}", [P, SLOT], F32R) for i in range(2)]
        wlo = [sb(f"wlo{i}", [P, SLOT], F32R) for i in range(2)]
        araw_off = top[0]
        araw = [sb(f"araw{i}", [P, D]) for i in range(2)]
        acc = sb("acc", [P, D])
        big = top[0]
        top[0] += 2 * KT * S * 4
        (h_hi, h_lo), _ = region(big, [("h_hi", [P, KT, S], F32R), ("h_lo", [P, KT, S], F32R)])
        (o_hi, o_lo), _ = region(big, [("o_hi", [P, KT, S], F32R), ("o_lo", [P, KT, S], F32R)])
        (f_hi, f_lo), _ = region(big, [("f_hi", [P, KT, S], F32R), ("f_lo", [P, KT, S], F32R)])
        (yout, gfb), _ = region(big, [("yout", [P, TB, D], F32), ("gfb", [P, D], F32)])
        mix = top[0]
        (mT, qk, convin, sigo, vT, V, Pt, Et, bc, md), end1 = region(mix, [
            ("mT", [P, 8, S], F32), ("qk", [P, 4, S], F32), ("convin", [P, 4, S + 4], F32),
            ("sigo", [P, 2, S], F32), ("vT", [P, 2, S], F32), ("V", [P, TB, HD + 1], F32),
            ("Pt", [P, 2, 5, P], F32), ("Et", [P, 5, P], F32), ("bc", [P, 2, S], F32), ("md", [P, 2, P], F32)])
        vT_off = mix + size([P, 8, S]) + size([P, 4, S]) + size([P, 4, S + 4]) + size([P, 2, S])
        (hm,), _ = region(vT_off, [("hm", [P, TB, HD], F32)])
        (xnT, xst0, xst1, hf), end0 = region(mix, [
            ("xnT", [P, KT, S], F32), ("xst0", [P, D], F32), ("xst1", [P, D], F32), ("hf", [P, 2, S], F32)])
        xst = [xst0, xst1]
        (stg, posi, ang, kf, ar2, junk), _ = region(big, [
            ("stg", [P, 3, P], F32), ("posi", [P, S], I32), ("ang", [P, S], F32), ("kf", [P, S], F32),
            ("ar2", [P, S], F32), ("junk", [P, D], F32)])
        (gsb, selI, selZ, li, zz, az, bb, aa, mx, blm, arow), end2 = region(mix, [
            ("gsb", [GATES, S], F32), ("selI", [GATES, 64], F32), ("selZ", [GATES, 64], F32),
            ("li", [64, S], F32), ("zz", [64, S], F32), ("az", [64, S], F32), ("bb", [64, S], F32),
            ("aa", [64, S], F32), ("mx", [64, S], F32), ("blm", [64, 16], F32), ("arow", [64, 10, P], F32)])
        (aout,), _ = region(mix, [("aout", [P, TB, AH * AD], F32)])
        (sc, pr, prT, sm, ajunk), _ = region(big + 8 * S * 4, [
            ("sc", [P, 2, 3 * P], F32), ("pr", [P, 2, 3 * P], F32), ("prT", [P, 2, 3 * P], F32),
            ("sm", [P, 32, 4], F32), ("ajunk", [P, AH * AD], F32)])
        (xT, xs0, xs1, sqt, ssum), end3 = region(mix, [
            ("xT", [P, KT, S], F32), ("xs0", [P, TB, S], F32), ("xs1", [P, TB, S], F32),
            ("sqt", [P, 2, S], F32), ("ssum", [P, S], F32)])
        (ht, hu), _ = region(mix + size([P, KT, S]), [("ht", [P, 2, S], F32), ("hu", [P, 2, S], F32)])
        (sqd,), _ = region(mix + size([P, KT, S]), [("sqd", [P, 4, S], F32)])
        xs = [xs0, xs1]
        a_hi = at("a_hi", [P, 4, S], F32R, araw_off)
        a_lo = at("a_lo", [P, 4, S], F32R, araw_off + 4 * S * 4)
        gs = at("gs", [P, 4, S], F32, araw_off + 8 * S * 4)

        assert max(end0, end1, end2, end3) <= 229344, (top[0], end0, end1, end2, end3)

        ps = [ctx.enter_context(nc.psum_tensor(f"ps{i}", [P, S], F32)) for i in range(8)]

        def sem(name):
            return ctx.enter_context(nc.semaphore(name))

        const_ld, x_ld, masks_ok, cst_T, cst_ok = map(sem, ["const_ld", "x_ld", "masks_ok", "cst_T", "cst_ok"])
        x_ld = [x_ld, sem("x_ld1")]
        ssq_ok, ms_ok, rsx_ok, xn_ok, xT_ps, xT_sb = map(
            sem, ["ssq_ok", "ms_ok", "rsx_ok", "xn_ok", "xT_ps", "xT_sb"])
        silu_sig, silu_ok, trig_in, trig_ok = map(sem, ["silu_sig", "silu_ok", "trig_in", "trig_ok"])
        ada_ld = [sem(f"ada_ld{i}") for i in range(4)]
        ada_acc, ada_sum, modp_ok, mod_ok = map(sem, ["ada_acc", "ada_sum", "modp_ok", "mod_ok"])
        hhi_ok, hlo_ok = map(sem, ["hhi_ok", "hlo_ok"])
        w_ld = [sem("w_ld0"), sem("w_ld1")]
        whi_ok, wlo_ok, w_used = map(sem, ["whi_ok", "wlo_ok", "w_used"])
        gate_sb, gate_sel, gate_rows, gate_exp, gate_ln, arow_ok, gcol_ps, gcol_sb, em_ok = map(
            sem, ["gate_sb", "gate_sel", "gate_rows", "gate_exp", "gate_ln", "arow_ok", "gcol_ps",
                  "gcol_sb", "em_ok"])
        proj_sb, conv_pre, conv_sig, conv_ok, vtr_ps, v_ok = map(
            sem, ["proj_sb", "conv_pre", "conv_sig", "conv_ok", "vtr_ps", "v_ok"])
        sel_ok, bc_ps, bc_sb, md_ok, s_ps, e_ok, p_ok, num_ps, num_used = map(
            sem, ["sel_ok", "bc_ps", "bc_sb", "md_ok", "s_ps", "e_ok", "p_ok", "num_ps", "num_used"])
        var_ok, rs_ok, hn_ok, ht_ps, mT_ok = map(sem, ["var_ok", "rs_ok", "hn_ok", "ht_ps", "mT_ok"])
        rot_ok, rope_ok = map(sem, ["rot_ok", "rope_ok"])
        as_ps, nm_ok, ex_ok, es_ok, pt_ps, pt_sb, pv_ps, ao_ok = map(
            sem, ["as_ps", "nm_ok", "ex_ok", "es_ok", "pt_ps", "pt_sb", "pv_ps", "ao_ok"])
        assq_ok, ams_ok, ars_ok, aon_ok, at_ps, ohi_ok, olo_ok, mhi_ok, mlo_ok = map(
            sem, ["assq_ok", "ams_ok", "ars_ok", "aon_ok", "at_ps", "ohi_ok", "olo_ok", "mhi_ok", "mlo_ok"])
        v_ld = [sem("v_ld0"), sem("v_ld1")]
        xs_ld = [sem("xs_ld0"), sem("xs_ld1")]
        vhi_ok, vlo_ok, v_used = map(sem, ["vhi_ok", "vlo_ok", "v_used"])
        c_sb, xl_sb, ct_ps, c_add, sq_ok, ssum_ok, sum_ok = map(
            sem, ["c_sb", "xl_sb", "ct_ps", "c_add", "sq_ok", "ssum_ok", "sum_ok"])
        n_ps, n_ms, n_rs, n_dg, n_bc, n_mul, fhi_ok, flo_ok = map(
            sem, ["n_ps", "n_ms", "n_rs", "n_dg", "n_bc", "n_mul", "fhi_ok", "flo_ok"])
        f_free, sig_ok, ahi_ok, alo_ok = map(sem, ["f_free", "sig_ok", "ahi_ok", "alo_ok"])
        yt_ps, y_sb, gf_ld, y_ok, y_okb, y_out = map(sem, ["yt_ps", "y_sb", "gf_ld", "y_ok", "y_okb", "y_out"])
        dve_chain, pool_chain = map(sem, ["dve_chain", "pool_chain"])

        NB = 45
        NC_ = 16
        XLOAD = (0, 3, 8, 11)
        RING0 = [wraw[0], wraw[1], araw[0], araw[1]]
        RING1 = [xst[0], xst[1], araw[0], araw[1]]
        BODY0 = [(0, 0), (1, 0), (2, 0), None, (0, 1), (1, 1), (2, 1), (3, 0), (3, 1)]
        ROPE = [convin[:, i, 2:2 + S] for i in range(4)] + [sigo[:, i, :] for i in range(2)] + \
               [qk[:, i, :] for i in range(4)]
        QH, KG = ROPE[2:], ROPE[:2]
        UNITS = [(n, h) for h in range(AH) for n in range(TB)]

        M_FROM = 6
        EARLY = 4
        SUM1, SUM2 = KT - 3, KT - 1
        SPLIT_AT = (8, 13)

        def c_bank(u):
            return 4 * ((u + 1) % 2)

        def blocks(n):
            return [k for k in (n - 1, n, n + 1) if 0 <= k < TB]

        TURN0 = ((4, 5, 6, 7), (4, 5, 4, 5))

        def tile_done(h, g, i):
            if isinstance(h, int) and h == 0:
                return 2 * BODY0.index((g, 1)) + 1 + i
            return h * 16 + (4 * g + 5 + i)

        def w3(t, k):
            return t[:].rearrange("p (k c) -> p k c", k=k)

        block = ctx.enter_context(nc.Block())

        @block.sync
        def _(sp):
            def rows(v, b=P):
                return v.rearrange("o (a b) -> (o a) b", b=b)

            for dst, src in ((stg[C_G1:C_G1 + 16, 0, :], rows(g1)), (stg[C_G2:C_G2 + 16, 0, :], rows(g2)),
                             (stg[C_GF:C_GF + 16, 0, :], gf.rearrange("(a b) -> a b", b=P)),
                             (stg[C_BC:C_BC + 16, 0, :], rows(b_conv)), (stg[C_GM:C_GM + 8, 0, :], rows(gm)),
                             (stg[C_GA:C_GA + 8, 0, :], rows(ga)), (stg[C_C:C_C + 16, 0, :], rows(c)),
                             (stg[0:96, 1, :], rows(b_ada)),
                             (stg[0:80, 2, :], w_conv.rearrange("o k (a b) -> (o k a) b", b=P)),
                             (sinkb[:], sink[0, :].partition_broadcast(P)),
                             (bgate[:], b_gates.rearrange("o g -> g o")),
                             (posi[:], positions[0, :].partition_broadcast(P)),
                             (invf[:], rope_inv)):
                sp.dma_start(dst, src).then_inc(const_ld, 16)

            def w_slot(par, s, col0, kk):
                if isinstance(s, int) and s < 2:
                    sp.wait_ge(ada_acc, 13 + s)
                else:
                    sp.wait_ge(wlo_ok, s - 1)
                sp.dma_start(w3(wraw[par], 8), w_in[0, kk * 1024:(kk + 1) * 1024, col0].rearrange(
                    "(k p) c -> p k c", p=P)).then_inc(w_ld[par], 16)

            def w_slot0(s):
                g, kk = BODY0[s]
                w_slot(s % 2, s, slice(g * 1024, g * 1024 + 256), kk)

            for n in range(32):
                ring = RING1 if n >= 16 else RING0
                if n >= 4:
                    sp.wait_ge(ada_acc, n - 3)
                if n in (16, 17):
                    sp.wait_ge(xT_ps, 4 * (n - 13))
                sp.dma_start(ring[n % 4][:].rearrange("p (q c) -> p q c", q=2),
                             w_ada[0, n % 16 * P:(n % 16 + 1) * P, 0:2 * D].rearrange(
                                 "p (q h c) -> p q h c", q=2, h=2)[:, :, n // 16, :]).then_inc(ada_ld[n % 4], 16)
                if n in XLOAD:
                    tb = XLOAD.index(n)
                    if tb >= 2:
                        sp.wait_ge(xT_ps, 4 * (tb - 1))
                    sp.dma_start(xst[tb % 2][:], x[0, tb * P:(tb + 1) * P, :]).then_inc(x_ld[tb % 2], 16)
                if n in (15, 17, 21):
                    w_slot0((15, 17, 21).index(n))
                if n == 25:
                    sp.wait_ge(wlo_ok, 2)
                    sp.dma_start(w3(wraw[1], 16), w_in[0, :, COL_G:COL_G + P].rearrange("(k p) c -> p k c", p=P))\
                        .then_inc(w_ld[1], 16)

            def ada_slot(par, m, q, kt):
                sp.wait_ge(ada_acc, 32 + m - 1)
                sp.dma_start(araw[par][:], w_ada[0, kt * P:(kt + 1) * P, q]).then_inc(ada_ld[2 + par], 16)

            def body(h, cols_of, q_cols, kt0, steps=8):
                for j in range(steps + 1):
                    if j < steps:
                        w_slot((1 + j) % 2, h * 8 + (1 + j), cols_of(j // 2), j % 2)
                    if j > 0:
                        ada_slot((j - 1) % 2, h * 8 + (j - 1), q_cols, kt0 + j - 1)

            for j, ms in enumerate(((0,), (1,), (), (), (2, 3, 4, 5, 6, 7))):
                w_slot0(4 + j)
                for m in ms:
                    ada_slot(m % 2, m, slice(2 * D, 3 * D), m)
            with sp.Fori(1, HEADS) as h:
                body(h, lambda g: bass.ds(h * 256 + g * 1024, 256), bass.ds(h * D + 2 * D, D), 0)
            tail = [COL_AK, COL_AQ, COL_AV, COL_AQ + 256]
            body(4, lambda g: slice(tail[g], tail[g] + 256), slice(2 * D, 3 * D), 8)
            for j in range(5):
                if j < 4:
                    col = COL_AQ + 512 + (j // 2) * 256
                    w_slot((1 + j) % 2, 41 + j, slice(col, col + 256), j % 2)
                for i in range(2 if j else 0):
                    ada_slot(i, 40 + 2 * (j - 1) + i, slice(3 * D, 4 * D), 8 + 2 * (j - 1) + i)

            def v_load(par, v, w, krow, col):
                if isinstance(v, int) and v < 2 + EARLY:
                    sp.wait_ge(wlo_ok, NB + max(v - 1, 0))
                else:
                    sp.wait_ge(vlo_ok, v - (EARLY + 1))
                sp.dma_start(w3(wraw[par], 4), w[0, krow, col].rearrange("(k p) c -> p k c", p=P))\
                    .then_inc(v_ld[par], 16)

            for v in range(NC_):
                u, ks = v // 4, v % 4
                v_load(v % 2, v, w_out, slice(ks * 512, ks * 512 + 512), slice(u * 512, u * 512 + 512))
                ada_slot(v % 2, 48 + v, slice((4 + v // 8) * D, (5 + v // 8) * D), 8 + v % 8)
                if ks == (2 if u else 3):
                    if u < 2:
                        sp.wait_ge(at_ps, 8)
                    else:
                        sp.wait_ge(ct_ps, u - 1)
                    sp.dma_start(xs[u % 2][:], x[0, :, u * 512:u * 512 + 512].rearrange("(b p) c -> p b c", p=P))\
                        .then_inc(xs_ld[u % 2], 16)

            def gu(v0, w, col):
                for ks in range(4):
                    v_load(ks % 2, v0 + ks, w, slice(ks * 512, ks * 512 + 512), col)

            def dn(v0, krow):
                for u in range(4):
                    v_load(u % 2, v0 + u, w_down, krow, slice(u * 512, u * 512 + 512))

            gu(16, w_gate, slice(0, CH))
            gu(20, w_up, slice(0, CH))
            with sp.Fori(0, NCH - 1) as i:
                gu(i * 12 + 24, w_gate, bass.ds(i * CH + CH, CH))
                dn(i * 12 + 28, bass.ds(i * CH, CH))
                gu(i * 12 + 32, w_up, bass.ds(i * CH + CH, CH))
            dn(NC_ + 8 + 12 * (NCH - 1), slice((NCH - 1) * CH, NCH * CH))
            sp.wait_ge(v_used, 4 * 144)
            sp.dma_start(gfb[:], gf.partition_broadcast(P)).then_inc(gf_ld, 16)
            for tb in range(TB):
                if tb < 2:
                    sp.wait_ge(y_ok, tb + 1)
                else:
                    sp.wait_ge(y_okb, tb - 1)
                sp.dma_start(out[0, tb * P:(tb + 1) * P, :], yout[:, tb, :]).then_inc(y_out, 16)
            sp.wait_ge(y_out, 16 * TB)

        @block.gpsimd
        def _(pool):
            ch = Chain(pool, pool_chain)
            ch.link(pool.memset(ident[:], 0.0))
            ch.link(pool.memset(mask3[:], 0.0))
            pool.affine_select(out=ident[:], in_=ident[:], compare_op=ALU.not_equal, fill=1.0, base=0,
                               pattern=[[-1, P]], channel_multiplier=1).then_inc(masks_ok, 1)
            pool.affine_select(out=mask_up, in_=mask_up, compare_op=ALU.is_ge, fill=NEG, base=0,
                               pattern=[[1, P]], channel_multiplier=-1).then_inc(masks_ok, 1)
            pool.affine_select(out=mask_lo, in_=mask_lo, compare_op=ALU.is_ge, fill=NEG, base=0,
                               pattern=[[-1, P]], channel_multiplier=1).then_inc(masks_ok, 1)
            pool.memset(ones[:], 1.0).then_inc(masks_ok, 1)
            ch.link(pool.memset(halfneg, -0.5))
            pool.memset(halfpi, np.pi / 2).then_inc(masks_ok, 1)

            for tb in range(TB):
                pool.wait_ge(ms_ok, tb + 1)
                pool.tensor_tensor(rsx[:, tb:tb + 1], rsx[:, tb:tb + 1], halfneg[:, 0:1], ALU.pow).then_inc(rsx_ok, 1)

            def lo(s, par):
                pool.wait_ge(whi_ok, s + 1)
                pool.tensor_tensor(wlo[par][:], wraw[par][:], whi[par][:].bitcast(F32), ALU.subtract)\
                    .then_inc(wlo_ok, 1)

            def body(h, mixing, steps=8, last=NB):
                for j in range(steps):
                    if not isinstance(h, int) or 3 + 8 * h + j < last:
                        lo(3 + 8 * h + j, (1 + j) % 2)
                    if mixing and j == 4:
                        pool.wait_ge(var_ok, h)
                        pool.tensor_tensor(rs, ve, halfneg, ALU.pow).then_inc(rs_ok, 1)

            for s in range(3):
                lo(s, s % 2)
            body(0, False)
            with pool.Fori(1, HEADS) as h:
                body(h, True)
            body(4, True)
            body(5, False, steps=4)

            def vlo(v):
                pool.wait_ge(vhi_ok, v + 1)
                pool.tensor_tensor(wlo[v % 2][:], wraw[v % 2][:], whi[v % 2][:].bitcast(F32), ALU.subtract)\
                    .then_inc(wlo_ok, 1)

            for v in range(3):
                vlo(v)
            pool.wait_ge(ams_ok, 1)
            pool.tensor_tensor(rs, ve, halfneg, ALU.pow).then_inc(ars_ok, 1)
            vlo(3)

            def add_squares(sq0, ss0, count):
                for n in range(count):
                    pool.wait_ge(sq_ok, sq0 + n + 1)
                    if n == 0:
                        pool.tensor_copy(ssum[:], sqt[:, 0, :]).then_inc(ssum_ok, 1)
                    else:
                        pool.wait_ge(ssum_ok, ss0 + n)
                        pool.tensor_tensor(ssum[:], ssum[:], sqt[:, n % 2, :], ALU.add).then_inc(ssum_ok, 1)

            add_squares(0, 0, SUM1)
            pool.wait_ge(n_ms, 1)
            pool.tensor_tensor(rs, ve, halfneg, ALU.pow).then_inc(n_rs, 1)
            add_squares(KT, SUM1, SUM2)
            pool.wait_ge(n_ms, 2)
            pool.tensor_tensor(rs, ve, halfneg, ALU.pow).then_inc(n_rs, 1)

        @block.scalar
        def _(act):
            A = nc.scalar.activation
            act.wait_ge(cst_ok, 1)
            A(tiny[:, 40:56], cols[:, C_C:C_C + 16], ACT.Sigmoid).then_inc(silu_sig, 1)
            for tb in range(TB):
                act.wait_ge(x_ld[tb % 2], 16 * (tb // 2 + 1))
                if tb:
                    act.wait_ge(ssq_ok, tb)
                A(junk[:], xst[tb % 2][:], ACT.Square, accum_out=ssq[:, tb:tb + 1]).then_inc(ssq_ok, 1)
                for q in range(4):
                    act.wait_ge(xT_ps, 4 * tb + q + 1)
                    A(xnT[:, 4 * q:4 * q + 4, tb * P:(tb + 1) * P],
                      ps[q % 2][:].rearrange("p (k t) -> p k t", k=4), ACT.Copy).then_inc(xT_sb, 1)
            act.wait_ge(trig_in, 1)
            A(sinT[:], ang[:], ACT.Sin, scale=invf[:, 1:2]).then_inc(trig_ok, 1)
            A(ar2[:], ang[:], ACT.Abs).then_inc(trig_ok, 1)
            act.wait_ge(trig_ok, 2)
            A(cosT[:], ar2[:], ACT.Sin, scale=-1.0, bias=halfpi).then_inc(trig_ok, 1)

            def hi(s, par, cnt):
                act.wait_ge(w_ld[par], 16 * cnt)
                A(whi[par][:], wraw[par][:], ACT.Copy).then_inc(whi_ok, 1)

            hi(0, 0, 1)
            act.wait_ge(trig_ok, 3)
            for half in range(2):
                act.wait_ge(mod_ok, half + 1)
                for kt in range(8 * half, 8 * half + 8):
                    A(h_hi[:, kt, :], xnT[:, kt, :], ACT.Identity, scale=mod[:, 1, kt:kt + 1],
                      bias=mod[:, 0, kt:kt + 1]).then_inc(hhi_ok, 1)
                if half == 0:
                    for s in (1, 2, 3, 4):
                        if s >= 2:
                            act.wait_ge(w_used, 2 * (s - 1))
                        hi(s, s % 2, s // 2 + 1)

            def gates():
                act.wait_ge(gate_rows, 1)
                A(az[:], az[:], ACT.Sigmoid).then_inc(gate_exp, 1)
                act.wait_ge(gate_exp, 1)
                A(az[:], az[:], ACT.Ln).then_inc(gate_ln, 1)

            def exp_minus_m():
                act.wait_ge(gcol_sb, 1)
                A(acol[:, 10 * GR:14 * GR], acol[:, 10 * GR:14 * GR], ACT.Exp, scale=-1.0).then_inc(em_ok, 1)

            def evac(dst, bank, n):
                act.wait_ge(w_used, n)
                A(dst, ps[bank][:], ACT.Copy).then_inc(proj_sb, 1)

            def o_gate(h, kind):
                if kind == "head" and not (isinstance(h, int) and h == 0):
                    act.wait_ge(mT_ok, h)
                elif kind == "tail":
                    act.wait_ge(mT_ok, 4)
                for i in range(2):
                    act.wait_ge(w_used, tile_done(h, 3, i))
                    A(sigo[:, i, :], ps[2 + i][:], ACT.Sigmoid if kind == "head" else ACT.Copy).then_inc(proj_sb, 1)

            def exps(m, i, base):
                act.wait_ge(md_ok, base + i + 1)
                if i:
                    act.wait_ge(p_ok, base + i)
                for j in range(i + 1):
                    col = PAIR[(i, j)] * GR
                    A(Et[:, j, :], md[:, 0, :] if j == i else bc[:, 0, i * P:(i + 1) * P], ACT.Exp, scale=-1.0,
                      bias=acol[:, bass.ds(m + col, 1)])
                for j in range(i, TB):
                    col = PAIR[(3 - i, 3 - j)] * GR + 32
                    last = A(Et[:, j + 1, :], md[:, 1, :] if j == i else bc[:, 1, i * P:(i + 1) * P], ACT.Exp,
                             scale=-1.0, bias=acol[:, bass.ds(m + col, 1)])
                last.then_inc(e_ok, 1)

            def rot(k):
                if k >= 2:
                    act.wait_ge(rope_ok, k - 1)
                act.wait_ge(proj_sb, (33, 34, 35, 36, 39, 40, 41, 42, 43, 44)[k])
                R = Pt[:, k % 2, 0:4, :].rearrange("p a b -> p (a b)")
                A(R[0:64, :], ROPE[k][64:P, :], ACT.Copy)
                A(R[64:P, :], ROPE[k][0:64, :], ACT.Copy).then_inc(rot_ok, 1)

            def body(h, kind, steps=8):
                mixing = kind in ("head", "tail")
                m = h - 1
                for j in range(steps):
                    s2 = h * 8 + (3 + j)
                    if kind == "first":
                        if j != 1 and j != 2:
                            s2 = 5 if j == 0 else s2
                            act.wait_ge(w_used, 2 * (s2 - 1))
                            hi(s2, s2 % 2, s2 // 2 + 1)
                    elif not isinstance(h, int) or s2 < NB:
                        act.wait_ge(w_used, h * 16 + (4 + 2 * j))
                        hi(s2, (3 + j) % 2, h * 4 + ((3 + j) // 2 + 1))
                    if j == 0 and kind != "first":
                        o_gate(m, "tail" if kind == "end" else "head")
                    if j == 0 and mixing:
                        for d in range(2):
                            act.wait_ge(bc_ps, h)
                            A(bc[:, d, :], ps[6 + d][:], ACT.Copy).then_inc(bc_sb, 1)
                    if j < 4 and mixing:
                        exps(m, j, m * 4)
                    if j == 0 and kind == "first":
                        gates()
                    if j == 5 and kind == "first":
                        for i in range(2):
                            evac(vT[:, i, :], 6 + i, tile_done(0, 2, i))
                        exp_minus_m()
                    if j == 2:
                        if kind == "head":
                            act.wait_ge(conv_ok, h * 4)
                        for i in range(2):
                            evac(qk[:, i, :] if kind == "end" else convin[:, i, 2:2 + S], i, tile_done(h, 0, i))
                    if j == 4:
                        for i in range(2):
                            evac(convin[:, 2 + i, 2:2 + S], 2 + i, tile_done(h, 1, i))
                    if kind in ("first", "head") and j in (5, 6):
                        for i in range(2):
                            t = 2 * (j - 5) + i
                            act.wait_ge(conv_pre, h * 4 + (t + 1))
                            A(Pt[:, i, 0:4, :].rearrange("p a b -> p (a b)"), qk[:, t, :], ACT.Sigmoid)\
                                .then_inc(conv_sig, 1)
                    if kind == "tail" and j in (5, 6):
                        if j == 5:
                            act.wait_ge(num_ps, 16)
                        rot(2 * (j - 5))
                        rot(2 * (j - 5) + 1)
                    if j == 6 and kind != "first":
                        if mixing:
                            act.wait_ge(ht_ps, h)
                        for i in range(2):
                            evac(vT[:, i, :], i, tile_done(h, 2, i))
                    if j == 7:
                        act.wait_ge(vtr_ps, h + 1)
                        for i in range(2):
                            A(V[:, 2 * i:2 * i + 2, 0:HD], ps[4 + i][:].rearrange("p (c e) -> p c e", c=2),
                              ACT.Copy).then_inc(v_ok, 1)
                    if kind == "end" and j in (1, 3):
                        rot(j + 3)
                        rot(j + 4)

            body(0, "first")
            with act.Fori(1, HEADS) as h:
                body(h, "head")
            body(4, "tail")
            body(5, "end", steps=4)
            for i in range(2):
                evac(qk[:, 2 + i, :], 2 + i, tile_done(5, 1, i))
            act.wait_ge(w_used, 2 * NB)

            def m_high(g):
                A(o_hi[:, 4 * g:4 * g + 4, :], mT[:, 4 * g:4 * g + 4, :], ACT.Copy).then_inc(mhi_ok, 1)

            def vhi(v, par, cnt, base=None):
                act.wait_ge(v_ld[par], cnt)
                A(whi[par][:], wraw[par][:], ACT.Copy).then_inc(vhi_ok, 1)

            def pt_copy(u):
                n, _ = UNITS[u]
                w = len(blocks(n)) * P
                act.wait_ge(pt_ps, u + 1)
                if u >= 2:
                    act.wait_ge(pv_ps, u - 1)
                A(prT[:, u % 2, 0:w], ps[2][:, 0:w], ACT.Copy).then_inc(pt_sb, 1)

            for u, (n, hh) in enumerate(UNITS):
                w = len(blocks(n)) * P
                act.wait_ge(nm_ok, u + 1)
                if u >= 2:
                    act.wait_ge(pt_ps, u - 1)
                A(pr[:, u % 2, 0:w], sc[:, u % 2, 0:w], ACT.Exp, scale=-1.0, bias=sm[:, u, 0:1],
                  accum_out=sm[:, u, 1:2]).then_inc(ex_ok, 1)
                A(sm[:, u, 2:3], sinkb[:, hh:hh + 1], ACT.Exp, bias=sm[:, u, 0:1]).then_inc(es_ok, 1)
                if u >= 1:
                    pt_copy(u - 1)
                if u in (0, 1):
                    m_high(u)
                elif u in (2, 4):
                    vhi(u // 2 - 1, u // 2 - 1, 16)
                elif u in (6, 7):
                    rot(u + 2)
                elif u == M_FROM + 18:
                    act.wait_ge(v_used, 4)
                    vhi(2, 0, 32)
            pt_copy(31)
            for n in range(TB):
                act.wait_ge(ao_ok, 29 + n)
                if n:
                    act.wait_ge(assq_ok, n)
                A(ajunk[:], aout[:, n, :], ACT.Square, accum_out=ssq[:, n:n + 1]).then_inc(assq_ok, 1)
            act.wait_ge(v_used, 8)
            vhi(3, 1, 32)
            for k in range(8):
                act.wait_ge(at_ps, k + 1)
                A(o_hi[:, 8 + k, :], ps[k % 4][:], ACT.Copy, scale=cols[:, C_GA + k:C_GA + k + 1]).then_inc(ohi_ok, 1)

            def squares(ss0, summed, n, ready, count):
                act.wait_ge(ready, count)
                if n >= summed:
                    dst = sqd[:, n - summed, :]
                else:
                    if n >= 2:
                        act.wait_ge(ssum_ok, ss0 + n - 1)
                    dst = sqt[:, n % 2, :]
                A(dst, xT[:, n, :], ACT.Square).then_inc(sq_ok, 1)

            for v in range(2, NC_):
                if v == NC_ - 1:
                    act.wait_ge(ct_ps, 4)
                    for i in range(4):
                        A(xT[:, 12 + i, :], ps[c_bank(2) + i][:], ACT.Copy).then_inc(xl_sb, 1)
                    for i in range(3):
                        squares(0, SUM1, 12 + i, c_add, 13 + i)
                act.wait_ge(v_used, 4 * v + 4)
                if v == NC_ - 1:
                    squares(0, SUM1, 15, c_add, 16)
                vhi(v + 2, v % 2, 16 * (v // 2 + 2))
                if v % 4 == 2 and v >= 4:
                    for i in range(4):
                        squares(0, SUM1, 4 * (v // 4 - 1) + i, c_add, 4 * (v // 4 - 1) + i + 1)

            def split_step(vb, k):
                act.wait_ge(v_used, vb * 4 + (4 * k + 4))
                par = k % 2
                act.wait_ge(v_ld[par], vb * 8 + 16 * (k // 2 + 2))
                A(whi[par][:], wraw[par][:], ACT.Copy).then_inc(vhi_ok, 1)

            for kt in range(KT):
                if kt in SPLIT_AT:
                    split_step(16, SPLIT_AT.index(kt))
                act.wait_ge(n_mul, kt + 1)
                A(f_hi[:, kt, :], ht[:, kt % 2, :], ACT.Identity, scale=mod[:, 4, kt:kt + 1],
                  bias=mod[:, 3, kt:kt + 1]).then_inc(fhi_ok, 1)

            def g_unit(v4, c4):
                for i in range(4):
                    act.wait_ge(v_used, v4 + (i + 1))
                    if isinstance(c4, int) and c4 == 0:
                        pass
                    else:
                        act.wait_ge(alo_ok, c4 + (i - 3))
                    A(gs[:, i, :], ps[i][:], ACT.Sigmoid).then_inc(sig_ok, 1)

            def u_unit(uu):
                for i in range(4):
                    act.wait_ge(f_free, uu * 4 + (i + 1))
                    A(a_hi[:, i, :], gs[:, i, :], ACT.Copy).then_inc(ahi_ok, 1)

            for k in range(2, 8):
                if k == 3:
                    g_unit(4 * 19, 0)
                if k == 7:
                    u_unit(1)
                split_step(16, k)
            with act.Fori(0, NCH - 1) as i:
                for k in range(12):
                    if k == 3:
                        g_unit(i * 48 + 4 * 27, i * 4 + 4)
                    if k == 11:
                        u_unit(i * 6 + 7)
                    split_step(i * 12 + 24, k)
            for k in range(4):
                if k < 2:
                    split_step(144, k)
                for i in range(4):
                    squares(SUM1, SUM2, 4 * k + i, f_free, 4 * 62 + 4 * k + i + 1)
            act.wait_ge(n_rs, 2)
            act.wait_ge(y_sb, KT)
            for tb in range(2, TB):
                A(yout[:, tb, :], yout[:, tb, :], ACT.Copy, scale=rs[:, tb:tb + 1]).then_inc(y_okb, 1)

        @block.vector
        def _(dve):
            V_ = nc.vector
            ch = Chain(dve, dve_chain)
            dve.wait_ge(cst_T, 1)
            V_.tensor_copy(cols[:, 0:C_WC + 80], ps[7][:, 0:C_END]).then_inc(cst_ok, 1)
            dve.wait_ge(silu_sig, 1)
            dve.wait_ge(cst_ok, 1)
            V_.tensor_tensor(csil[:], cols[:, C_C:C_C + 16], tiny[:, 40:56], ALU.mult).then_inc(silu_ok, 1)
            dve.wait_ge(silu_ok, 1)

            def ada_op(n, slot, ld, cnt, kt, first):
                dve.wait_ge(ada_ld[ld], cnt)
                if first:
                    V_.tensor_scalar(acc[:], slot[:], csil[:, kt:kt + 1], None, ALU.mult).then_inc(ada_acc, 1)
                else:
                    dve.wait_ge(ada_acc, n)
                    V_.scalar_tensor_tensor(out=acc[:], in0=slot[:], scalar=csil[:, kt:kt + 1], in1=acc[:],
                                            op0=ALU.mult, op1=ALU.add).then_inc(ada_acc, 1)

            def ada_take(n, which, bank):
                dve.wait_ge(ada_sum, n + 1)
                j = 4 * (n % 4)
                V_.tensor_reduce(modp[:, which, j:j + 4], ps[bank][:].rearrange("p (a b) -> p a b", a=4), AX.X, ALU.add)\
                    .then_inc(modp_ok, 1)

            def ada_take0(half):
                for b in range(4):
                    dve.wait_ge(ada_sum, 8 * half + 2 * (b + 1))
                    for t in range(2):
                        j = 8 * half + 4 * (b % 2) + 2 * t
                        V_.tensor_reduce(modp[:, b // 2, j:j + 2], ps[TURN0[half][b]][:, 2 * t * P:(2 * t + 2) * P].rearrange(
                            "p (a b) -> p a b", a=2), AX.X, ALU.add).then_inc(modp_ok, 1)

            def mean_square(tb):
                dve.wait_ge(ssq_ok, tb + 1)
                V_.tensor_scalar(rsx[:, tb:tb + 1], ssq[:, tb:tb + 1], 1.0 / D, EPS, ALU.mult, ALU.add)\
                    .then_inc(ms_ok, 1)

            def normalise(tb):
                dve.wait_ge(rsx_ok, tb + 1)
                V_.tensor_scalar(xst[tb % 2][:], xst[tb % 2][:], rsx[:, tb:tb + 1], None, ALU.mult)\
                    .then_inc(xn_ok, 1)

            def trig():
                dve.wait_ge(const_ld, 16 * 13)
                ch.link(V_.tensor_copy(ang[:], posi[:]))
                ch.link(V_.tensor_scalar(ang[:], ang[:], invf[:, 0:1], None, ALU.mult))

            def trig_round(scale):
                ch.link(V_.tensor_scalar(kf[:], ang[:], 1.0 / (TWO_PI * scale), MAGIC, ALU.mult, ALU.add))
                ch.link(V_.tensor_scalar(kf[:], kf[:], -MAGIC, None, ALU.add))
                for part in (PI_1, PI_2, PI_3):
                    ch.link(V_.scalar_tensor_tensor(out=ang[:], in0=kf[:], scalar=-part * scale, in1=ang[:],
                                                    op0=ALU.mult, op1=ALU.add))

            def trig_end():
                V_.tensor_scalar(ang[:], ang[:], PI_SAFE, -PI_SAFE, ALU.min, ALU.max).then_inc(trig_in, 1)

            def add_bias(q):
                ch.link(V_.tensor_tensor(mod[:, q, :], modp[:, q, :], modp[:, q + 6, :], ALU.add))
                ch.link(V_.tensor_tensor(mod[:, q, :], mod[:, q, :], cols[:, C_BA + 16 * q:C_BA + 16 * q + 16], ALU.add))

            def scale_gain(q, g, part=slice(0, KT)):
                return (V_.scalar_tensor_tensor(out=mod[:, q, part], in0=mod[:, q, part], scalar=1.0,
                                                in1=cols[:, g + part.start:g + part.stop], op0=ALU.add, op1=ALU.mult))

            def h_float(kt):
                if kt >= 2:
                    dve.wait_ge(hlo_ok, kt - 1)
                ch.link(V_.tensor_scalar(hf[:, kt % 2, :], xnT[:, kt, :], mod[:, 1, kt:kt + 1],
                                         mod[:, 0, kt:kt + 1], ALU.mult, ALU.add))

            def h_half(half):
                ada_take0(half)
                part = slice(8 * half, 8 * half + 8)
                dve.wait_ge(modp_ok, 8 * half + 8)
                for q in range(2):
                    last = V_.tensor_tensor(mod[:, q, part], modp[:, q, part],
                                            cols[:, C_BA + 16 * q + part.start:C_BA + 16 * q + part.stop], ALU.add)
                ch.link(last)
                scale_gain(1, C_G1, part).then_inc(mod_ok, 1)
                dve.wait_ge(mod_ok, half + 1)
                dve.wait_ge(xT_sb, 16)
                h_float(part.start)
                for kt in range(part.start, part.stop):
                    if kt + 1 < part.stop:
                        h_float(kt + 1)
                    dve.wait_ge(hhi_ok, kt + 1)
                    V_.tensor_tensor(h_lo[:, kt, :], hf[:, kt % 2, :], h_hi[:, kt, :].bitcast(F32), ALU.subtract)\
                        .then_inc(hlo_ok, 1)
                    if half == 0 and kt % 2:
                        ada0(16 + kt // 2)

            def ada0(n):
                slot = (RING1 if n >= 16 else RING0)[n % 4]
                ada_op(n, slot, n % 4, 16 * (n // 4 + 1), n % 16, n % 16 == 0)

            for n in [*range(16), *range(20, 32)]:
                ada0(n)
                if n - 2 in XLOAD:
                    mean_square(XLOAD.index(n - 2))
                if n - 3 in XLOAD:
                    normalise(XLOAD.index(n - 3))
                if n == 2:
                    trig()
                if n == 3:
                    trig_round(2048.0)
                if n == 4:
                    trig_round(1.0)
                    trig_end()
                if n % 16 == 15:
                    h_half(n // 16)

            ch.link(V_.memset(convin[:, :, 0:2], 0.0))
            ch.link(V_.memset(convin[:, :, S + 2:S + 4], 0.0))
            ch.link(V_.memset(V[:, :, HD:HD + 1], 1.0))
            ch.link(V_.memset(selI[:], 0.0))
            ch.link(V_.memset(selZ[:], 0.0))
            for dst, src in ((selI[:, 0:4], 0), (selI[:, 32:36], 8), (selZ[:, 0:4], 4), (selZ[:, 32:36], 12)):
                ch.link(V_.tensor_copy(dst, ident[0:GATES, src:src + 4]))

            def gates_in():
                dve.wait_ge(w_used, 8)
                V_.tensor_scalar(gsb[:], ps[4][0:GATES, :], bgate[:, 0:1], None, ALU.add).then_inc(gate_sb, 1)

            def gate_rows_():
                dve.wait_ge(gate_sel, 1)
                for dst, bank in ((li, 5), (zz, 4)):
                    ch.link(V_.tensor_copy(dst[0:32, :], ps[bank][0:32, :]))
                    ch.link(V_.tensor_copy(dst[32:64, :], ps[bank][32:64, ::-1]))
                V_.scalar_tensor_tensor(out=az[:], in0=zz[:], scalar=-1.0, in1=zz[:], op0=ALU.mult, op1=ALU.max)\
                    .then_inc(gate_rows, 1)
                dve.wait_ge(gate_rows, 1)
                ch.link(V_.tensor_scalar(zz[:], zz[:], 0.0, None, ALU.min))
                ch.link(V_.memset(blm[:, 0:1], 0.0))
                dve.wait_ge(gate_ln, 1)
                ch.link(V_.tensor_tensor(zz[:], zz[:], az[:], ALU.add))

                def chunk(j):
                    return slice(j * P, (j + 1) * P)

                for j in range(TB):
                    ch.link(V_.tensor_tensor_scan(bb[:, chunk(j)], ones[0:64, :], zz[:, chunk(j)], 0.0,
                                                  ALU.mult, ALU.add))
                ch.link(V_.tensor_tensor(aa[:], li[:], bb[:], ALU.subtract))
                for j in range(TB):
                    ch.link(V_.tensor_tensor_scan(mx[:, chunk(j)], aa[:, chunk(j)], aa[:, chunk(j)],
                                                  blm[:, j:j + 1], ALU.max, ALU.max))
                    e = (j + 1) * P - 1
                    ch.link(V_.tensor_tensor(blm[:, j + 1:j + 2], bb[:, e:e + 1], mx[:, e:e + 1], ALU.add))
                ch.link(V_.tensor_copy(mnat[0:32, :], mx[0:32, :]))
                ch.link(V_.tensor_copy(mnat[32:64, :], mx[32:64, ::-1]))
                ch.link(V_.tensor_tensor(az[0:32, :], bb[0:32, :], mx[0:32, :], ALU.add))
                ch.link(V_.tensor_tensor(az[32:64, :], bb[32:64, ::-1], mx[32:64, ::-1], ALU.add))
                for j in range(TB):
                    for i in range(j, TB):
                        k = PAIR[(i, j)]
                        bl = bb[:, i * P - 1:i * P] if i else None
                        off = blm[:, 8:9]
                        if i == j + 1:
                            ch.link(V_.tensor_copy(off, bl))
                        elif i > j:
                            ch.link(V_.tensor_tensor(off, off, bl, ALU.add))
                        back = aa[32:64, chunk(j)][:, ::-1]
                        if i == j:
                            ch.link(V_.tensor_copy(arow[0:32, k, :], aa[0:32, chunk(j)]))
                            ch.link(V_.tensor_copy(arow[32:64, k, :], back))
                        else:
                            ch.link(V_.tensor_scalar(arow[0:32, k, :], aa[0:32, chunk(j)], off[0:32], None, ALU.add))
                            ch.link(V_.tensor_scalar(arow[32:64, k, :], back, off[32:64], None, ALU.add))
                V_.tensor_copy(arow[0:1, 0, 0:1], arow[0:1, 0, 0:1]).then_inc(arow_ok, 1)

            def gate_columns():
                dve.wait_ge(gcol_ps, 1)
                V_.tensor_copy(acol[:], ps[5][:, 0:14 * GR]).then_inc(gcol_sb, 1)

            def select(h):
                if not (isinstance(h, int) and h == 0):
                    dve.wait_ge(bc_ps, h)
                for d in range(2):
                    last = V_.tensor_copy(sel2[:, d, :], ident[0:64, bass.ds(h + 32 * d, 1)].to_broadcast([64, P]))
                last.then_inc(sel_ok, 1)

            def diag(m, j):
                if j == 0:
                    dve.wait_ge(bc_sb, m * 2 + 2)
                if j:
                    dve.wait_ge(e_ok, m * 4 + j)
                V_.tensor_tensor(md[:, 0, :], bc[:, 0, j * P:(j + 1) * P], mask_up, ALU.subtract)
                V_.tensor_tensor(md[:, 1, :], bc[:, 1, j * P:(j + 1) * P], mask_lo, ALU.subtract).then_inc(md_ok, 1)

            def weigh(m, j):
                dve.wait_ge(s_ps, m * 4 + (j + 1))
                dve.wait_ge(e_ok, m * 4 + (j + 1))
                if j >= 2:
                    dve.wait_ge(num_ps, m * 4 + (j - 1))
                S3 = ps[4][:].rearrange("p (c t) -> p c t", c=TB)
                V_.tensor_tensor(Pt[:, j % 2, 0:j + 1, :], S3[:, 0:j + 1, :], Et[:, 0:j + 1, :], ALU.mult)
                V_.tensor_tensor(Pt[:, j % 2, j + 1:5, :], S3[:, j:TB, :], Et[:, j + 1:5, :], ALU.mult)\
                    .then_inc(p_ok, 1)

            def combine(m, j):
                if isinstance(m, int) and m == 0 and j == 0:
                    dve.wait_ge(em_ok, 1)
                dve.wait_ge(num_ps, m * 4 + (j + 1))
                for d in range(2):
                    den = ps[6 + d][:, HD:HD + 1]
                    ch.link(V_.tensor_scalar(dd[:, d:d + 1], den, -1.0,
                                             acol[:, bass.ds(m + ((10 + j) * GR + 32 * d), 1)], ALU.mult, ALU.max))
                    ch.link(V_.tensor_tensor(dd[:, d:d + 1], dd[:, d:d + 1], den, ALU.max))
                ch.link(V_.reciprocal(rr, dd))
                ch.link(V_.tensor_scalar(hm[:, j, :], ps[6][:, 0:HD], rr[:, 0:1], None, ALU.mult))
                V_.scalar_tensor_tensor(out=hm[:, j, :], in0=ps[7][:, 0:HD], scalar=rr[:, 1:2], in1=hm[:, j, :],
                                        op0=ALU.mult, op1=ALU.add).then_inc(num_used, 1)
                dve.wait_ge(num_used, m * 4 + (j + 1))
                ch.link(V_.bn_stats(st6, hm[:, j, :]))
                V_.tensor_copy(tiny[:, 56:57], rr[:, 0:1])
                ch.link(V_.bn_aggr(mv[:, 2 * j:2 * j + 2], st6))
                if j == TB - 1:
                    V_.tensor_scalar(ve, mv.rearrange("p (c k) -> p c k", k=2)[:, :, 1], EPS, None, ALU.add)\
                        .then_inc(var_ok, 1)

            def layer_norm(m):
                dve.wait_ge(rs_ok, m + 1)
                for j in range(TB):
                    last = V_.tensor_scalar(hm[:, j, :], hm[:, j, :], mv[:, 2 * j:2 * j + 1], rs[:, j:j + 1],
                                            ALU.subtract, ALU.mult)
                last.then_inc(hn_ok, 1)

            def mlstm_out(m):
                dve.wait_ge(ht_ps, m + 1)
                dve.wait_ge(proj_sb, m * 8 + 8)
                for d in range(2):
                    last = V_.scalar_tensor_tensor(
                        out=mT[:, bass.ds(m * 2 + d, 1), :].rearrange("p a t -> p (a t)"), in0=ps[4 + d][:],
                        scalar=cols[:, bass.ds(m * 2 + (C_GM + d), 1)], in1=sigo[:, d, :], op0=ALU.mult, op1=ALU.mult)
                last.then_inc(mT_ok, 1)

            def conv(h, t):
                dve.wait_ge(proj_sb, h * 8 + (2 if t < 2 else 4))
                tile = h * 2 + (t if t < 2 else 6 + t)
                ch.link(V_.tensor_scalar(qk[:, t, :], convin[:, t, 0:S], cols[:, bass.ds(tile + C_WC, 1)],
                                         cols[:, bass.ds(tile + C_BC, 1)], ALU.mult, ALU.add))
                for k in range(1, CONV):
                    ins = V_.scalar_tensor_tensor(out=qk[:, t, :], in0=convin[:, t, k:k + S],
                                                  scalar=cols[:, bass.ds(tile + (C_WC + 16 * k), 1)],
                                                  in1=qk[:, t, :], op0=ALU.mult, op1=ALU.add)
                    if k < CONV - 1:
                        ch.link(ins)
                ins.then_inc(conv_pre, 1)

            def silu(h, t):
                dve.wait_ge(conv_sig, h * 4 + (t + 1))
                V_.scalar_tensor_tensor(out=qk[:, t, :], in0=qk[:, t, :], scalar=1.0 if t < 2 else HD ** -0.5,
                                        in1=Pt[:, t % 2, 0:4, :].rearrange("p a b -> p (a b)"),
                                        op0=ALU.mult, op1=ALU.mult).then_inc(conv_ok, 1)

            def rope(k):
                dve.wait_ge(rot_ok, k + 1)
                if k == 0:
                    dve.wait_ge(trig_ok, 3)
                R = Pt[:, k % 2, 0:4, :].rearrange("p a b -> p (a b)")
                ch.link(V_.tensor_tensor(ROPE[k], ROPE[k], cosT[:], ALU.mult))
                ch.link(V_.tensor_tensor(R, R, sinT[:], ALU.mult))
                V_.tensor_tensor(ROPE[k], ROPE[k], R, ALU.add).then_inc(rope_ok, 1)

            def ada_b(par, m_base, j, kt, first, cnt):
                dve.wait_ge(ada_ld[2 + par], cnt)
                if first:
                    V_.tensor_scalar(acc[:], araw[par][:], csil[:, kt:kt + 1], None, ALU.mult).then_inc(ada_acc, 1)
                else:
                    dve.wait_ge(ada_acc, m_base + (32 + j))
                    V_.scalar_tensor_tensor(out=acc[:], in0=araw[par][:], scalar=csil[:, kt:kt + 1], in1=acc[:],
                                            op0=ALU.mult, op1=ALU.add).then_inc(ada_acc, 1)

            def ada_part(h, kind, j):
                which = h + 2 if kind != "tail" else 2 + 6
                for b in range(2):
                    dve.wait_ge(ada_sum, h * 4 + (17 + 2 * (j - 6) + b))
                    q = 4 * (2 * (j - 6) + b)
                    V_.tensor_reduce(modp[:, bass.ds(which, 1), q:q + 4].rearrange("p a k -> p (a k)"),
                                     ps[6 + b][:].rearrange("p (a b) -> p a b", a=4), AX.X, ALU.add)\
                        .then_inc(modp_ok, 1)

            def body(h, kind, steps=8):
                mixing = kind in ("head", "tail")
                m = h - 1
                for j in range(steps):
                    if kind == "first" and j == 5:
                        gate_columns()
                    for i in (range(2 * j, 2 * j + 2) if kind == "end" else
                              {0: (), 1: (0, 1), 2: (2,), 3: (3,), 4: (4, 5), 5: (6, 7)}.get(j, ())):
                        if kind == "end":
                            ada_b(i % 2, 40, i, 8 + i, i == 0, 16 * (8 + 20 + i // 2 + 1))
                        else:
                            ada_b(i % 2, h * 8, i, i if kind != "tail" else 8 + i, i == 0,
                                  h * 64 + 16 * (8 + i // 2 + 1))
                    if kind == "first" and j == 0:
                        gates_in()
                        gate_rows_()
                    if mixing and j < 4:
                        diag(m, j)
                    if mixing and 1 <= j <= 4:
                        combine(m, j - 1)
                    if mixing and j < 4:
                        weigh(m, j)
                    if mixing and j == 5:
                        layer_norm(m)
                    if mixing and j == 6:
                        mlstm_out(m)
                    if kind == "first" and j == 6:
                        ada_part(h, kind, j)
                    if kind in ("first", "head") and j in (5, 6):
                        t = 2 * (j - 5)
                        conv(h, t)
                        conv(h, t + 1)
                        silu(h, t)
                        silu(h, t + 1)
                    if kind == "tail" and j in (5, 6):
                        rope(2 * (j - 5))
                        rope(2 * (j - 5) + 1)
                    if kind == "end" and j == 1:
                        rope(4)
                        rope(5)
                    if kind in ("first", "head") and j == 7:
                        select(h)
                    if kind != "end" and j in (6, 7) and (kind, j) != ("first", 6):
                        ada_part(h, kind, j)

            body(0, "first")
            LINKS = 8 * TB + 4 * 4
            with dve.Fori(1, HEADS) as h:
                ch.enter(h, 1, LINKS)
                body(h, "head")
            ch.leave(HEADS - 1)
            body(4, "tail")
            body(5, "end", steps=4)
            ch.link(V_.tensor_scalar(nsink[:], sinkb[:], -1.0, None, ALU.mult))

            def vlo(v_hi, par):
                dve.wait_ge(vhi_ok, v_hi)
                V_.tensor_tensor(wlo[par][:], wraw[par][:], whi[par][:].bitcast(F32), ALU.subtract)\
                    .then_inc(vlo_ok, 1)


            def softmax_in(u):
                n, hh = UNITS[u]
                bl = blocks(n)
                w = len(bl) * P
                m0 = (bl[0] - n + 1) * P
                dve.wait_ge(as_ps, u + 1)
                if u >= 2:
                    dve.wait_ge(ex_ok, u - 1)
                V_.tensor_tensor_reduce(out=sc[:, u % 2, 0:w], in0=ps[u % 2][:, 0:w], in1=mask3[:, m0:m0 + w],
                                        scale=-AD ** -0.5, scalar=nsink[:, hh:hh + 1], op0=ALU.add, op1=ALU.min,
                                        accum_out=sm[:, u, 0:1]).then_inc(nm_ok, 1)

            ROPE_AT = {5: 6, 7: 7, 9: 8, 10: 9}

            def head_out(u):
                n, hh = UNITS[u]
                dve.wait_ge(es_ok, u + 1)
                ch.link(V_.tensor_tensor(sm[:, u, 3:4], sm[:, u, 1:2], sm[:, u, 2:3], ALU.add))
                ch.link(V_.reciprocal(sm[:, u, 3:4], sm[:, u, 3:4]))
                dve.wait_ge(pv_ps, u + 1)
                if hh == 0 and n == 0:
                    dve.wait_ge(mlo_ok, 2)
                V_.tensor_scalar(aout[:, n, hh * AD:(hh + 1) * AD], ps[3][:, 0:AD], sm[:, u, 3:4], None,
                                 ALU.mult).then_inc(ao_ok, 1)

            for u in range(32):
                softmax_in(u)
                if u >= 3:
                    head_out(u - 3)
                if u in (1, 2):
                    g = u - 1
                    dve.wait_ge(mhi_ok, g + 1)
                    V_.tensor_tensor(o_lo[:, 4 * g:4 * g + 4, :], mT[:, 4 * g:4 * g + 4, :],
                                     o_hi[:, 4 * g:4 * g + 4, :].bitcast(F32), ALU.subtract).then_inc(mlo_ok, 1)
                elif u == 3:
                    for b in range(4):
                        ada_take(36 + b, 3 + 6, 4 + b)
                elif u == 4:
                    dve.wait_ge(modp_ok, 40)
                    add_bias(2)
                elif u in ROPE_AT:
                    rope(ROPE_AT[u])
                elif u in (12, 16, 20, 24):
                    v = u // 4 - 3
                    ada_b(v % 2, 48, v, 8 + v, v == 0, 16 * (8 + 24 + v // 2 + 1))
            for u in range(29, 32):
                head_out(u)
            dve.wait_ge(assq_ok, TB)
            V_.tensor_scalar(ve, ssq, 1.0 / (AH * AD), EPS, ALU.mult, ALU.add).then_inc(ams_ok, 1)
            dve.wait_ge(ars_ok, 1)
            for n in range(TB):
                V_.tensor_scalar(aout[:, n, :], aout[:, n, :], rs[:, n:n + 1], None, ALU.mult).then_inc(aon_ok, 1)
            for k in range(8):
                dve.wait_ge(ohi_ok, k + 1)
                V_.scalar_tensor_tensor(out=o_lo[:, 8 + k, :], in0=ps[k % 4][:], scalar=cols[:, C_GA + k:C_GA + k + 1],
                                        in1=o_hi[:, 8 + k, :].bitcast(F32), op0=ALU.mult, op1=ALU.subtract)\
                    .then_inc(olo_ok, 1)

            def add_x(u):
                dve.wait_ge(ct_ps, u + 1)
                for i in range(4):
                    V_.tensor_tensor(xT[:, 4 * u + i, :], xT[:, 4 * u + i, :], ps[c_bank(u) + i][:], ALU.add)\
                        .then_inc(c_add, 1)

            for v in range(2, NC_):
                u = v // 4
                if v >= 4:
                    ada_b(v % 2, 48, v, 8 + v % 8, v % 8 == 0, 16 * (8 + 24 + v // 2 + 1))
                if v == 7:
                    for b in range(4):
                        ada_take(40 + b, 4 + 6, 4 + b)
                if v % 4 == 2 and v >= 4:
                    add_x(u - 1)
                if v % 4 == 3 and u < 3:
                    for i in range(4):
                        dve.wait_ge(v_used, 4 * v + i + 1)
                        V_.tensor_scalar(xT[:, 4 * u + i, :], ps[c_bank(u) + i][:], mod[:, 2, 4 * u + i:4 * u + i + 1],
                                         None, ALU.mult).then_inc(c_sb, 1)
                if v < NC_ - 1:
                    vlo(v + 3, v % 2)

            def join_squares(n, sq, done=False):
                if n == 0:
                    dve.wait_ge(ssum_ok, sq)
                else:
                    dve.wait_ge(sq_ok, sq)
                ins = V_.tensor_tensor(sqd[:, 0, :], sqd[:, 0, :], sqd[:, n, :] if n else ssum[:], ALU.add)
                if done:
                    ins.then_inc(sum_ok, 1)
                else:
                    ch.link(ins)

            for i in range(4):
                dve.wait_ge(xl_sb, i + 1)
                dve.wait_ge(v_used, 4 * NC_ - 3 + i)
                V_.scalar_tensor_tensor(out=xT[:, 12 + i, :], in0=ps[c_bank(3) + i][:], scalar=mod[:, 2, 12 + i:13 + i],
                                        in1=xT[:, 12 + i, :], op0=ALU.mult, op1=ALU.add).then_inc(c_add, 1)
                if i == 2:
                    dve.wait_ge(sq_ok, SUM1 + 1)
                    join_squares(0, SUM1)
                    join_squares(1, 15)
            join_squares(2, KT, done=True)
            for b in range(3):
                ada_take(44 + b, 5 + 6, 4 + b)

            def mean_squares(k):
                dve.wait_ge(n_ps, k)
                V_.tensor_scalar(ve, ps[0][:, 0:4], 1.0 / D, EPS, ALU.mult, ALU.add).then_inc(n_ms, 1)

            mean_squares(1)
            ada_take(47, 5 + 6, 7)
            dve.wait_ge(n_rs, 1)
            for tb in range(TB):
                last = V_.tensor_scalar(sqt[:, 0, tb * P:(tb + 1) * P], ident[:], rs[:, tb:tb + 1], None, ALU.mult)
            last.then_inc(n_dg, 1)
            dve.wait_ge(modp_ok, 48)
            for q in (3, 4, 5):
                add_bias(q)
            ch.link(scale_gain(4, C_G2))
            dve.wait_ge(n_bc, 1)

            def split_step(vb, k):
                dve.wait_ge(vhi_ok, vb + (k + 3))
                V_.tensor_tensor(wlo[k % 2][:], wraw[k % 2][:], whi[k % 2][:].bitcast(F32), ALU.subtract)\
                    .then_inc(vlo_ok, 1)

            for kt in range(KT):
                if kt == 2:
                    vlo(NC_ + 2, 1)
                if kt in SPLIT_AT:
                    split_step(16, SPLIT_AT.index(kt))
                if kt >= 2:
                    dve.wait_ge(fhi_ok, kt - 1)
                V_.tensor_tensor(ht[:, kt % 2, :], xT[:, kt, :], ps[7][:], ALU.mult).then_inc(n_mul, 1)
                dve.wait_ge(n_mul, kt + 1)
                ch.link(V_.tensor_scalar(hu[:, kt % 2, :], ht[:, kt % 2, :], mod[:, 4, kt:kt + 1],
                                         mod[:, 3, kt:kt + 1], ALU.mult, ALU.add))
                dve.wait_ge(fhi_ok, kt + 1)
                V_.tensor_tensor(f_lo[:, kt, :], hu[:, kt % 2, :], f_hi[:, kt, :].bitcast(F32), ALU.subtract)\
                    .then_inc(flo_ok, 1)

            def g_unit(c4):
                for i in range(4):
                    dve.wait_ge(sig_ok, c4 + (i + 1))
                    V_.tensor_tensor(gs[:, i, :], ps[i][:], gs[:, i, :], ALU.mult).then_inc(f_free, 1)

            def u_unit(v4, uu, c4):
                dve.wait_ge(f_free, uu * 4)
                for i in range(4):
                    dve.wait_ge(v_used, v4 + (i + 1))
                    V_.tensor_tensor(gs[:, i, :], ps[4 + i][:], gs[:, i, :], ALU.mult).then_inc(f_free, 1)
                    dve.wait_ge(ahi_ok, c4 + (i + 1))
                    V_.tensor_tensor(a_lo[:, i, :], gs[:, i, :], a_hi[:, i, :].bitcast(F32), ALU.subtract)\
                        .then_inc(alo_ok, 1)

            def d_tile(v4, u, bank, i):
                t = 4 * u + i
                dve.wait_ge(v_used, v4 + (i + 1))
                V_.scalar_tensor_tensor(out=xT[:, t, :], in0=ps[bank + i][:], scalar=mod[:, 5, t:t + 1],
                                        in1=xT[:, t, :], op0=ALU.mult, op1=ALU.add).then_inc(f_free, 1)

            for k in range(2, 8):
                if k == 3:
                    g_unit(0)
                if k == 7:
                    u_unit(4 * 23, 1, 0)
                split_step(16, k)
            with dve.Fori(0, NCH - 1) as i:
                for k in range(12):
                    if k == 3:
                        g_unit(i * 4 + 4)
                    if 4 <= k < 8:
                        if k == 4:
                            dve.wait_ge(f_free, i * 24 + 12)
                        for t in range(4):
                            d_tile(i * 48 + 4 * (24 + k), k - 4, 4 * ((k + 1) % 2), t)
                    if k == 11:
                        u_unit(i * 48 + 4 * 35, i * 6 + 7, i * 4 + 4)
                    split_step(i * 12 + 24, k)
            dve.wait_ge(f_free, 4 * 62)

            def y_tile(u, i):
                t = 4 * u + i
                dve.wait_ge(yt_ps, 4 * u + i + 1)
                V_.tensor_tensor(yout[:, :, t * P:(t + 1) * P],
                                 ps[4 * (u % 2) + i][:].rearrange("p (b f) -> p b f", b=TB),
                                 gfb[:, t * P:(t + 1) * P].unsqueeze(1).to_broadcast([P, TB, P]), ALU.mult)\
                    .then_inc(y_sb, 1)

            for u in range(4):
                for i in range(4):
                    d_tile(4 * (144 + u), u, 4 * (u % 2), i)
                    if i == 1 and u:
                        if u == 1:
                            dve.wait_ge(gf_ld, 16)
                        for k in range(4):
                            y_tile(u - 1, k)
                if u < 2:
                    split_step(144, u)
            y_tile(3, 0)
            dve.wait_ge(sq_ok, 2 * KT)
            join_squares(0, SUM1 + SUM2, done=True)
            for k in range(1, 4):
                y_tile(3, k)
            mean_squares(2)
            dve.wait_ge(n_rs, 2)
            dve.wait_ge(y_sb, KT)
            for tb in range(2):
                V_.tensor_scalar(yout[:, tb, :], yout[:, tb, :], rs[:, tb:tb + 1], None, ALU.mult).then_inc(y_ok, 1)

        @block.tensor
        def _(pe):
            def mm3(o, w_hi, w_lo, m_hi, m_lo, first, last):
                pe.matmul(o, w_hi, m_hi, start=first, stop=False)
                pe.matmul(o, w_hi, m_lo, start=False, stop=False)
                return pe.matmul(o, w_lo, m_hi, start=False, stop=last)

            pe.wait_ge(const_ld, 16 * 13)
            pe.wait_ge(masks_ok, 5)
            for i, (n, off) in enumerate(((96, 0), (96, C_BA), (80, C_WC))):
                last = pe.transpose(ps[7][:, off:off + n], stg[0:n, i, :], ident[0:n, 0:n])
            last.then_inc(cst_T, 1)

            def x_block(tb):
                pe.wait_ge(xn_ok, tb + 1)
                for q in range(4):
                    if 4 * tb + q >= 2:
                        pe.wait_ge(xT_sb, 4 * tb + q - 1)
                    for i in range(4):
                        f = 4 * q + i
                        last = pe.transpose(ps[q % 2][:, i * P:(i + 1) * P], xst[tb % 2][:, f * P:(f + 1) * P], ident[:])
                    last.then_inc(xT_ps, 1)

            def ada_turn(hidx, banks, j0=0):
                if j0 == 0:
                    pe.wait_ge(ada_acc, hidx * 8 + 8)
                for b, bank in enumerate(banks):
                    for i in range(4):
                        j = 4 * (j0 + b) + i
                        last = pe.transpose(ps[bank][:, i * P:(i + 1) * P], acc[:, j * P:(j + 1) * P], ident[:])
                    last.then_inc(ada_sum, 1)

            pe.wait_ge(cst_ok, 1)
            for tb in range(TB):
                x_block(tb)

            def ada_turn0(half):
                pe.wait_ge(ada_acc, 16 * (half + 1))
                for b in range(4):
                    bank = TURN0[half][b]
                    if half and b >= 2:
                        pe.wait_ge(modp_ok, 8 + 2 * (b - 1))
                    for i in range(4):
                        j = 4 * b + i
                        ins = pe.transpose(ps[bank][:, i * P:(i + 1) * P], acc[:, j * P:(j + 1) * P], ident[:])
                        if i >= 2:
                            ins.then_inc(ada_sum, 1)

            def part0(s, i, kts, bank, done=True):
                _, kk = BODY0[s]
                for kt in kts:
                    pe.wait_ge(hlo_ok, kt + 1)
                    k = kt % 8
                    last = mm3(ps[bank][:], w3(whi[s % 2], 8)[:, k, i * P:(i + 1) * P],
                               w3(wlo[s % 2], 8)[:, k, i * P:(i + 1) * P], h_hi[:, kt, :], h_lo[:, kt, :],
                               kt == 0, kt == KT - 1)
                if done:
                    last.then_inc(w_used, 1)

            def slot0(s):
                g, kk = BODY0[s]
                pe.wait_ge(wlo_ok, s + 1)
                for i in range(2):
                    if (g, kk) == (3, 0):
                        pe.wait_ge(proj_sb, 3 + i)
                    part0(s, i, range(8 * kk, 8 * kk + 8), (0, 2, 6, 2)[g] + i)
                    if s == 4 and i == 0:
                        gate_select()

            ada_turn0(0)
            pe.wait_ge(wlo_ok, 1)
            for kt in range(8):
                for i in range(2):
                    part0(0, i, (kt,), i, done=(kt == 7))
            slot0(1)
            slot0(2)
            ada_turn0(1)
            pe.wait_ge(wlo_ok, 4)
            pe.wait_ge(modp_ok, 16)
            for kt in range(KT):
                pe.wait_ge(hlo_ok, kt + 1)
                last = mm3(ps[4][:], w3(whi[1], 16)[:, kt, :], w3(wlo[1], 16)[:, kt, :], h_hi[:, kt, :], h_lo[:, kt, :],
                           kt == 0, kt == KT - 1)
                if kt in (7, 15):
                    last.then_inc(w_used, 1)

            def slot(h, j):
                par, g, kk = (1 + j) % 2, j // 2, j % 2
                pe.wait_ge(wlo_ok, h * 8 + (2 + j))
                for i in range(2):
                    bank = 2 * (g % 2) + i
                    if kk == 0:
                        pe.wait_ge(proj_sb, h * 8 + (2 * g + i - 3))
                    for k in range(8):
                        last = mm3(ps[bank][:], w3(whi[par], 8)[:, k, i * P:(i + 1) * P],
                                   w3(wlo[par], 8)[:, k, i * P:(i + 1) * P], h_hi[:, 8 * kk + k, :],
                                   h_lo[:, 8 * kk + k, :], kk == 0 and k == 0, kk == 1 and k == 7)
                    last.then_inc(w_used, 1)

            def gate_select():
                pe.wait_ge(gate_sb, 1)
                pe.matmul(ps[5][0:64, :], selI[:], gsb[:], start=True, stop=True)
                pe.matmul(ps[4][0:64, :], selZ[:], gsb[:], start=True, stop=True).then_inc(gate_sel, 1)

            def gate_columns():
                pe.wait_ge(arow_ok, 1)
                for k in range(14):
                    src = arow[:, k, :] if k < 10 else az[:, (k - 10) * P:(k - 9) * P]
                    last = pe.matmul(ps[5][:, k * GR:(k + 1) * GR], src, ident[0:64, 0:GR], start=True, stop=True)
                last.then_inc(gcol_ps, 1)

            def spread_m(m):
                pe.wait_ge(sel_ok, m + 1)
                pe.wait_ge(modp_ok, m * 4 + 20)
                for d in range(2):
                    last = pe.matmul(ps[6 + d][:], sel2[:, d, :], mnat[:], start=True, stop=True)
                last.then_inc(bc_ps, 1)

            def scores(m, i):
                if i == 0:
                    pe.wait_ge(conv_ok, m * 4 + 4)
                    pe.wait_ge(v_ok, m * 2 + 2)
                else:
                    pe.wait_ge(p_ok, m * 4 + i)
                for j in range(TB):
                    for d in range(2):
                        last = pe.matmul(ps[4][:, j * P:(j + 1) * P], qk[:, 2 + d, j * P:(j + 1) * P],
                                         qk[:, d, i * P:(i + 1) * P], start=(d == 0), stop=(d == 1))
                last.then_inc(s_ps, 1)

            def numerators(m, i):
                pe.wait_ge(p_ok, m * 4 + (i + 1))
                if i == 0:
                    pe.wait_ge(bc_sb, m * 2 + 2)
                else:
                    pe.wait_ge(num_used, m * 4 + i)
                for j in range(i + 1):
                    pe.matmul(ps[6][:, 0:HD + 1], Pt[:, i % 2, j, :], V[:, j, :], start=(j == 0), stop=(j == i))
                for j in range(i, TB):
                    last = pe.matmul(ps[7][:, 0:HD + 1], Pt[:, i % 2, j + 1, :], V[:, j, :], start=(j == i),
                                     stop=(j == TB - 1))
                last.then_inc(num_ps, 1)

            def turn_h(m):
                pe.wait_ge(hn_ok, m + 1)
                for d in range(2):
                    for i in range(TB):
                        last = pe.transpose(ps[4 + d][:, i * P:(i + 1) * P], hm[:, i, d * P:(d + 1) * P], ident[:])
                last.then_inc(ht_ps, 1)

            def turn_v(h, mixing):
                pe.wait_ge(proj_sb, h * 8 + 6)
                if mixing:
                    pe.wait_ge(mT_ok, h)
                for i in range(TB):
                    for d in range(2):
                        last = pe.transpose(ps[4 + i // 2][:, (i % 2) * HD + d * P:(i % 2) * HD + (d + 1) * P],
                                            vT[:, d, i * P:(i + 1) * P], ident[:])
                last.then_inc(vtr_ps, 1)

            def body(h, kind, steps=8):
                mixing = kind in ("head", "tail")
                m = h - 1
                for j in range(steps):
                    if kind != "first":
                        slot(h, j)
                    elif j >= 3:
                        slot0(1 + j)
                    if kind == "first" and j == 5:
                        gate_columns()
                    if mixing and j == 0:
                        spread_m(m)
                    if mixing and 1 <= j <= 4:
                        numerators(m, j - 1)
                    if mixing and j < 4:
                        scores(m, j)
                    if j == 6 and mixing:
                        pe.wait_ge(num_used, h * 4)
                        turn_h(m)
                    if j == 7 and kind == "first":
                        pe.wait_ge(gcol_sb, 1)
                        pe.wait_ge(proj_sb, 6)
                    if j == (7 if kind == "first" else 6):
                        ada_turn(h + 4, (6, 7))
                    if j == 7:
                        if kind == "first":
                            turn_v(h, mixing)
                        pe.wait_ge(modp_ok, h * 4 + 18)
                        ada_turn(h + 4, (6, 7), 2)
                        if kind != "first":
                            turn_v(h, mixing)
                if kind == "end":
                    pe.wait_ge(modp_ok, 36)
                    pe.wait_ge(v_ok, 10)
                    ada_turn(9, (4, 5, 6, 7))

            body(0, "first")
            with pe.Fori(1, HEADS) as h:
                body(h, "head")
            body(4, "tail")
            body(5, "end", steps=4)

            def att_scores(u):
                n, hh = UNITS[u]
                pe.wait_ge(rope_ok, hh + 3)
                if u == 0:
                    pe.wait_ge(proj_sb, 44)
                if u >= 2:
                    pe.wait_ge(nm_ok, u - 1)
                bl = blocks(n)
                pe.matmul(ps[u % 2][:, 0:len(bl) * P], QH[hh][:, n * P:(n + 1) * P],
                          KG[hh // 4][:, bl[0] * P:(bl[-1] + 1) * P], start=True, stop=True).then_inc(as_ps, 1)

            def att_turn(u):
                n, hh = UNITS[u]
                pe.wait_ge(ex_ok, u + 1)
                if u >= 1:
                    pe.wait_ge(pt_sb, u)
                for b in range(len(blocks(n))):
                    last = pe.transpose(ps[2][:, b * P:(b + 1) * P], pr[:, u % 2, b * P:(b + 1) * P], ident[:])
                last.then_inc(pt_ps, 1)

            def att_values(u):
                n, hh = UNITS[u]
                g = hh // 4
                bl = blocks(n)
                pe.wait_ge(pt_sb, u + 1)
                if u == 0:
                    pe.wait_ge(v_ok, 10)
                else:
                    pe.wait_ge(ao_ok, u)
                for b, k in enumerate(bl):
                    last = pe.matmul(ps[3][:, 0:AD], prT[:, u % 2, b * P:(b + 1) * P],
                                     V[:, k, g * AD:(g + 1) * AD], start=(b == 0), stop=(b == len(bl) - 1))
                last.then_inc(pv_ps, 1)

            def m_piece(n):
                v, i, k = n // 16, n // 4 % 4, n % 4
                if n == 0:
                    pe.wait_ge(mlo_ok, 2)
                    pe.wait_ge(modp_ok, 40)
                if n % 16 == 0:
                    pe.wait_ge(wlo_ok, NB + v + 1)
                last = mm3(ps[c_bank(0) + i][:], w3(whi[v], 4)[:, k, i * P:(i + 1) * P],
                           w3(wlo[v], 4)[:, k, i * P:(i + 1) * P], o_hi[:, 4 * v + k, :], o_lo[:, 4 * v + k, :],
                           v == 0 and k == 0, False)
                if k == 3:
                    last.then_inc(v_used, 1)

            att_scores(0)
            att_scores(1)
            piece = 0
            for u in range(32):
                att_turn(u)
                if u + 2 < 32:
                    att_scores(u + 2)
                if u >= M_FROM:
                    m_piece(piece)
                    piece += 1
                if u >= 1:
                    att_values(u - 1)
            att_values(31)
            while piece < 32:
                m_piece(piece)
                piece += 1
            pe.wait_ge(ao_ok, 32)
            pe.wait_ge(aon_ok, TB)
            for k in range(8):
                if k >= 4:
                    pe.wait_ge(olo_ok, k - 3)
                for n in range(TB):
                    last = pe.transpose(ps[k % 4][:, n * P:(n + 1) * P], aout[:, n, k * P:(k + 1) * P], ident[:])
                last.then_inc(at_ps, 1)

            def turn_x(u, bank=None):
                pe.wait_ge(xs_ld[u % 2], 16 * (u // 2 + 1))
                if bank is None:
                    bank = c_bank(u)
                    pe.wait_ge(c_sb, 4 * (u + 1))
                for i in range(4):
                    for tb in range(TB):
                        last = pe.transpose(ps[bank + i][:, tb * P:(tb + 1) * P],
                                            xs[u % 2][:, tb, i * P:(i + 1) * P], ident[:])
                last.then_inc(ct_ps, 1)

            def vslot(par, v, o, m_hi, m_lo, k0, first, last_, bank_free=None, tile_ready=None):
                if isinstance(v, int) and v < EARLY:
                    pe.wait_ge(wlo_ok, NB + v + 1)
                else:
                    pe.wait_ge(vlo_ok, v + (1 - EARLY))
                for i in range(4):
                    if bank_free is not None:
                        pe.wait_ge(*bank_free(i))
                    for k in range(4):
                        if tile_ready is not None and i == 0:
                            pe.wait_ge(*tile_ready(k))
                        last = mm3(ps[o + i][:], w3(whi[par], 4)[:, k, i * P:(i + 1) * P],
                                   w3(wlo[par], 4)[:, k, i * P:(i + 1) * P], m_hi[:, k0 + k, :], m_lo[:, k0 + k, :],
                                   first and k == 0, last_ and k == 3)
                    last.then_inc(v_used, 1)

            for v in range(2, NC_):
                u, ks = v // 4, v % 4
                free = ready = None
                if u == 0:
                    ready = lambda k, v=v: (olo_ok, 4 * (v - 2) + k + 1)
                elif ks == 0 and u == 1:
                    free = lambda i: (olo_ok, 4 + i + 1)
                elif ks == 0:
                    free = lambda i, u=u: (c_add, 4 * (u - 2) + i + 1)
                    if u == 2:
                        pe.wait_ge(modp_ok, 44)
                vslot(v % 2, v, c_bank(u), o_hi, o_lo, 4 * ks, ks == 0, ks == 3, free, ready)
                if ks == 1 and u:
                    turn_x(u - 1)
                if v == 7:
                    pe.wait_ge(c_add, 4)
                    ada_turn(10, (4, 5, 6, 7))
                if v == 14:
                    pe.wait_ge(c_add, 12)
                    turn_x(3, c_bank(2))

            def sum_columns(k):
                pe.wait_ge(sum_ok, k)
                for tb in range(TB):
                    last = pe.matmul(ps[0][:, tb:tb + 1], sqd[:, 0, tb * P:(tb + 1) * P], ones[:, 0:1], start=True, stop=True)
                last.then_inc(n_ps, 1)

            pe.wait_ge(xl_sb, 4)
            ada_turn(11, (4, 5, 6, 7))
            pe.wait_ge(c_add, 16)
            sum_columns(1)
            pe.wait_ge(modp_ok, 48)
            pe.wait_ge(n_dg, 1)
            for tb in range(TB):
                last = pe.matmul(ps[7][:, tb * P:(tb + 1) * P], ones[:], sqt[:, 0, tb * P:(tb + 1) * P], start=True, stop=True)
            last.then_inc(n_bc, 1)
            for ks in range(4):
                pe.wait_ge(vlo_ok, 17 + ks - EARLY)
                for k in range(4):
                    pe.wait_ge(flo_ok, 4 * ks + k + 1)
                    for i in range(4):
                        last = mm3(ps[i][:], w3(whi[ks % 2], 4)[:, k, i * P:(i + 1) * P],
                                   w3(wlo[ks % 2], 4)[:, k, i * P:(i + 1) * P], f_hi[:, 4 * ks + k, :],
                                   f_lo[:, 4 * ks + k, :], ks == 0 and k == 0, ks == 3 and k == 3)
                        if k == 3:
                            last.then_inc(v_used, 1)
            for ks in range(4):
                vslot(ks % 2, 20 + ks, 4, f_hi, f_lo, 4 * ks, ks == 0, ks == 3)

            def unit_free(uu):
                return lambda i: (f_free, uu * 4 + (i - 7))

            with pe.Fori(0, NCH - 1) as i:
                for k in range(4):
                    vslot(k % 2, i * 12 + (24 + k), 0, f_hi, f_lo, 4 * k, k == 0, k == 3,
                          unit_free(i * 6 + 2) if k == 0 else None)
                pe.wait_ge(alo_ok, i * 4 + 4)
                for k in range(4, 8):
                    vslot(k % 2, i * 12 + (24 + k), 4 * ((k + 1) % 2), a_hi, a_lo, 0, True, True, unit_free(i * 6 + (k - 1)))
                for k in range(8, 12):
                    vslot(k % 2, i * 12 + (24 + k), 4, f_hi, f_lo, 4 * (k - 8), k == 8, k == 11,
                          unit_free(i * 6 + 7) if k == 8 else None)

            def turn_y(u):
                for i in range(4):
                    pe.wait_ge(f_free, 4 * 62 + 4 * u + i + 1)
                    for tb in range(TB):
                        last = pe.transpose(ps[4 * (u % 2) + i][:, tb * P:(tb + 1) * P],
                                            xT[:, 4 * u + i, tb * P:(tb + 1) * P], ident[:])
                    last.then_inc(yt_ps, 1)

            pe.wait_ge(alo_ok, 4 * NCH)
            for u in range(4):
                par = u % 2
                pe.wait_ge(vlo_ok, 145 + u - EARLY)
                for i in range(4):
                    if u < 2:
                        pe.wait_ge(f_free, 4 * (60 + u) + i + 1)
                    else:
                        pe.wait_ge(y_sb, 4 * (u - 2) + i + 1)
                    for k in range(4):
                        last = mm3(ps[4 * (u % 2) + i][:], w3(whi[par], 4)[:, k, i * P:(i + 1) * P],
                                   w3(wlo[par], 4)[:, k, i * P:(i + 1) * P], a_hi[:, k, :], a_lo[:, k, :], k == 0, k == 3)
                    last.then_inc(v_used, 1)
                    if i == 1 and u:
                        turn_y(u - 1)
            turn_y(3)
            pe.wait_ge(y_sb, 9)
            sum_columns(2)


_INS = ["x", "c", "positions", "w_ada", "b_ada", "g_norm1", "g_norm2", "w_in", "b_gates", "w_conv", "b_conv",
        "g_mlstm_out", "sink", "g_attn_out", "w_out", "w_gate", "w_up", "w_down", "g_final"]


def rope_constants():
    half = AD // 2
    inv = (10000.0 ** (-np.arange(half) * 2.0 / AD)).astype(np.float32)
    t = np.empty((P, 2), np.float32)
    t[:half, 0] = inv
    t[half:, 0] = inv
    t[:half, 1] = -1.0
    t[half:, 1] = 1.0
    return t


def kernel(**inputs):
    import concourse.bacc as _bacc
    from concourse.bass_utils import run_bass_kernel_spmd as _run

    nc = _bacc.Bacc("TRN2", target_bir_lowering=False, num_devices=1)
    arrays, args = {}, []
    for name in _INS:
        a = np.ascontiguousarray(inputs[name])
        arrays[f"in_{name}"] = a
        args.append(nc.dram_tensor(f"in_{name}", a.shape, mybir.dt.from_np(a.dtype), kind="ExternalInput").ap())
    t = rope_constants()
    arrays["rope_constants"] = t
    args.append(nc.dram_tensor("rope_constants", t.shape, F32, kind="ExternalInput").ap())
    args.append(nc.dram_tensor("out", (1, S, D), F32, kind="ExternalOutput").ap())
    program(nc, *args)
    r = _run(nc, [arrays], core_ids=[0])
    return r.results[0]["out"]
```
